# Optimizing a Trainium2 kernel written in Bass

```python
import jax, jax.numpy as jnp
from jax import lax
import numpy as np
import jax
import jax.numpy as jnp

D_MODEL = 1024
BATCH = 1
SEQ = 256
DEPTH = 2

GRID_W = 64
CTX_LEN = 256
N_EVEN = (DEPTH + 1) // 2
N_ODD = DEPTH // 2
RMS_EPS = 1e-6

POOL_WIDTH = D_MODEL // 2
POOL_WINDOWS = (2, 4, 8, 16)
POOL_GROUP = POOL_WIDTH // len(POOL_WINDOWS)
HG_WIDTH = D_MODEL // 2
HG_HEAD_DIM = 128
HG_HEADS = HG_WIDTH // HG_HEAD_DIM
HG_CHUNK = 64
AB_IN = POOL_WIDTH + 5 * HG_WIDTH
AB_MIX = POOL_WIDTH + HG_WIDTH
ATT_HEAD_DIM = 128
ATT_HEADS = D_MODEL // ATT_HEAD_DIM
ATT_KV_HEADS = 2
ATT_GROUP = ATT_HEADS // ATT_KV_HEADS
ATT_IN = (ATT_HEADS + 2 * ATT_KV_HEADS) * ATT_HEAD_DIM
Q_BLOCK = 128
ROPE_THETA = 10000.0
FFN_HIDDEN = ((8 * D_MODEL + 3 * 256 - 1) // (3 * 256)) * 256


F32 = jnp.float32

def rmsnorm(x, g):
    xf = x.astype(F32)
    y = xf * lax.rsqrt(jnp.mean(xf * xf, axis=-1, keepdims=True) + RMS_EPS)
    return (y * g.astype(F32)).astype(x.dtype)

def flip(a):
    return a[:, ::-1]

def swiglu(h, w_in, w_out):
    a, b = jnp.split(h @ w_in, 2, axis=-1)
    return (jax.nn.silu(a) * b) @ w_out

def grid_rope(x):
    L = x.shape[1]
    rows = L // GRID_W
    row = jnp.repeat(jnp.arange(rows, dtype=F32), GRID_W)
    col = jnp.tile(jnp.arange(GRID_W, dtype=F32), rows)
    n_freq = ATT_HEAD_DIM // 4
    inv = ROPE_THETA ** (-jnp.arange(n_freq, dtype=F32) / n_freq)

    def rot(xa, pos):
        ang = pos[:, None] * inv[None, :]
        cos = jnp.cos(ang)[:, None, :]
        sin = jnp.sin(ang)[:, None, :]
        x1, x2 = jnp.split(xa, 2, axis=-1)
        return jnp.concatenate([x1 * cos - x2 * sin, x2 * cos + x1 * sin], axis=-1)

    xf = x.astype(F32)
    half = ATT_HEAD_DIM // 2
    return jnp.concatenate([rot(xf[..., :half], row), rot(xf[..., half:], col)], axis=-1).astype(x.dtype)

def multiscale_pool(u, pool_w, pool_scale):
    Bn, Ln, _ = u.shape
    cs = jnp.pad(jnp.cumsum(u.astype(F32), axis=1), ((0, 0), (1, 0), (0, 0)))
    t = jnp.arange(Ln)
    groups = []
    for gi, w in enumerate(POOL_WINDOWS):
        lo = jnp.clip(t - w // 2, 0, Ln)
        hi = jnp.clip(t - w // 2 + w, 0, Ln)
        sl = slice(gi * POOL_GROUP, (gi + 1) * POOL_GROUP)
        csg = cs[..., sl]
        mean = (csg[:, hi] - csg[:, lo]) / (hi - lo).astype(F32)[None, :, None]
        groups.append(mean - u[..., sl].astype(F32))
    y = jnp.stack(groups, axis=2).astype(u.dtype)
    y = jnp.einsum('blgc,gcd->blgd', y, pool_w).reshape(Bn, Ln, POOL_WIDTH)
    return y * pool_scale

def hgrn_scan(q, k, v, logf, s0):
    Bn, Ln, H, _ = q.shape
    dv = v.shape[-1]
    n = Ln // HG_CHUNK

    def chunks(a):
        return jnp.moveaxis(a.reshape(Bn, n, HG_CHUNK, H, a.shape[-1]), 1, 0)

    causal = jnp.tril(jnp.ones((HG_CHUNK, HG_CHUNK), dtype=bool))[None, :, :, None, None]

    def step(S, inp):
        qc, kc, vc, gc = inp
        b = jnp.cumsum(gc, axis=1)
        dec = jnp.exp(jnp.where(causal, b[:, :, None] - b[:, None, :], -jnp.inf))
        a = jnp.einsum('bthd,btshd->btsh', qc, dec * kc[:, None])
        o = jnp.einsum('btsh,bshe->bthe', a, vc) + jnp.einsum('bthd,bhde->bthe', qc * jnp.exp(b), S)
        b_last = b[:, -1]
        S = jnp.exp(b_last)[..., None] * S + jnp.einsum('bshd,bshe->bhde', kc * jnp.exp(b_last[:, None] - b), vc)
        return S, o

    s_fin, o = lax.scan(step, s0, (chunks(q), chunks(k), chunks(v), chunks(logf)))
    return jnp.moveaxis(o, 0, 1).reshape(Bn, Ln, H, dv), s_fin

def pool_hgrn_mixer(h_lat, h_ctx, w_in, w_out, pool_w, pool_scale, lb, onorm_g, need_ctx):
    def project(h):
        z = h @ w_in
        Bn, Ln = z.shape[:2]
        u = z[..., :POOL_WIDTH]
        q, zf, zb, v, g = jnp.split(z[..., POOL_WIDTH:], 5, axis=-1)
        heads = lambda a: a.reshape(Bn, Ln, HG_HEADS, HG_HEAD_DIM).astype(F32)
        return u, heads(jax.nn.silu(q)), heads(zf), heads(zb), heads(v), g

    def gate(z, lb_dir):
        f = lb_dir + (1.0 - lb_dir) * jax.nn.sigmoid(z)
        return 1.0 - f, jnp.log(f)

    lb_f = lb[0].reshape(HG_HEADS, HG_HEAD_DIM)
    lb_b = lb[1].reshape(HG_HEADS, HG_HEAD_DIM)
    u_c, q_c, zf_c, zb_c, v_c, g_c = project(h_ctx)
    u_l, q_l, zf_l, zb_l, v_l, g_l = project(h_lat)
    k_cf, lf_cf = gate(zf_c, lb_f)
    k_cb, lf_cb = gate(zb_c, lb_b)
    k_lf, lf_lf = gate(zf_l, lb_f)
    k_lb, lf_lb = gate(zb_l, lb_b)

    s0 = jnp.zeros((h_ctx.shape[0], HG_HEADS, HG_HEAD_DIM, HG_HEAD_DIM), F32)
    o_cf, s_f = hgrn_scan(q_c, k_cf, v_c, lf_cf, s0)
    o_cb, s_b = hgrn_scan(flip(q_c), flip(k_cb), flip(v_c), flip(lf_cb), s0)
    o_lf, _ = hgrn_scan(q_l, k_lf, v_l, lf_lf, s_f)
    o_lb, _ = hgrn_scan(flip(q_l), flip(k_lb), flip(v_l), flip(lf_lb), s_b)

    def readout(o_sum, g, u):
        Bn, Ln = g.shape[:2]
        o = rmsnorm(o_sum, onorm_g).reshape(Bn, Ln, HG_WIDTH).astype(g.dtype) * jax.nn.silu(g)
        return jnp.concatenate([multiscale_pool(u, pool_w, pool_scale), o], axis=-1) @ w_out

    y_lat = readout(o_lf + flip(o_lb), g_l, u_l)
    y_ctx = readout(o_cf + flip(o_cb), g_c, u_c) if need_ctx else None
    return y_lat, y_ctx

def gqa_mixer(h_lat, h_ctx, w_in, w_out, qn_g, kn_g, need_ctx):
    dh = ATT_HEAD_DIM

    def project(h):
        z = h @ w_in
        Bn, Ln = z.shape[:2]
        q = z[..., :ATT_HEADS * dh].reshape(Bn, Ln, ATT_HEADS, dh)
        k = z[..., ATT_HEADS * dh:(ATT_HEADS + ATT_KV_HEADS) * dh].reshape(Bn, Ln, ATT_KV_HEADS, dh)
        v = z[..., (ATT_HEADS + ATT_KV_HEADS) * dh:].reshape(Bn, Ln, ATT_KV_HEADS, dh)
        return rmsnorm(q, qn_g), rmsnorm(k, kn_g), v

    Bn, L, _ = h_lat.shape
    Lc = h_ctx.shape[1]
    q_l, k_l, v_l = project(h_lat)
    q_c, k_c, v_c = project(h_ctx)
    q_l = grid_rope(q_l)
    k_l = grid_rope(k_l)
    k_all = jnp.concatenate([k_l, k_c], axis=1)
    v_all = jnp.concatenate([v_l, v_c], axis=1)
    scale = dh ** -0.5

    def attend(qb, k, v):
        s = jnp.einsum('bqhgd,bkhd->bhgqk', qb, k, preferred_element_type=F32) * scale
        p = jax.nn.softmax(s, axis=-1).astype(v.dtype)
        return jnp.einsum('bhgqk,bkhd->bqhgd', p, v)

    q_blocks = jnp.moveaxis(q_l.reshape(Bn, L // Q_BLOCK, Q_BLOCK, ATT_KV_HEADS, ATT_GROUP, dh), 1, 0)
    o = lax.map(lambda qb: attend(qb, k_all, v_all), q_blocks)
    y_lat = jnp.moveaxis(o, 0, 1).reshape(Bn, L, ATT_HEADS * dh) @ w_out
    y_ctx = None
    if need_ctx:
        o_c = attend(q_c.reshape(Bn, Lc, ATT_KV_HEADS, ATT_GROUP, dh), k_c, v_c)
        y_ctx = o_c.reshape(Bn, Lc, ATT_HEADS * dh) @ w_out
    return y_lat, y_ctx

def first_inputs(seed: int = 0) -> dict:
    key = jax.random.key(seed)
    ks = jax.random.split(key, 20)
    D = D_MODEL
    nrm = lambda k, shape, s: jax.random.normal(k, shape, F32) * s
    return {
        "x": nrm(ks[0], (BATCH, SEQ, D), 1.0),
        "c": nrm(ks[1], (BATCH, D), 1.0),
        "ctx": nrm(ks[2], (BATCH, CTX_LEN, D), 1.0),
        "c_ctx": nrm(ks[3], (D,), 1.0),
        "ada_w": nrm(ks[4], (DEPTH, D, 6 * D), 0.5 * D ** -0.5),
        "ada_b": nrm(ks[5], (DEPTH, 6 * D), 0.02),
        "norm_g": 1.0 + nrm(ks[6], (DEPTH, 4, D), 0.02),
        "ab_w_in": nrm(ks[7], (N_EVEN, D, AB_IN), D ** -0.5),
        "ab_w_out": nrm(ks[8], (N_EVEN, AB_MIX, D), AB_MIX ** -0.5),
        "pool_w": nrm(ks[9], (N_EVEN, len(POOL_WINDOWS), POOL_GROUP, POOL_GROUP), POOL_GROUP ** -0.5),
        "pool_scale": 1.0 + nrm(ks[10], (N_EVEN, POOL_WIDTH), 0.1),
        "hg_lower": nrm(ks[11], (N_EVEN + 1, 2, HG_WIDTH), 0.1),
        "hg_onorm_g": 1.0 + nrm(ks[12], (N_EVEN, HG_HEAD_DIM), 0.02),
        "att_w_in": nrm(ks[13], (N_ODD, D, ATT_IN), D ** -0.5),
        "att_w_out": nrm(ks[14], (N_ODD, ATT_HEADS * ATT_HEAD_DIM, D), (ATT_HEADS * ATT_HEAD_DIM) ** -0.5),
        "att_qnorm_g": 1.0 + nrm(ks[15], (N_ODD, ATT_HEAD_DIM), 0.02),
        "att_knorm_g": 1.0 + nrm(ks[16], (N_ODD, ATT_HEAD_DIM), 0.02),
        "ffn_w_in": nrm(ks[17], (DEPTH, D, 2 * FFN_HIDDEN), D ** -0.5),
        "ffn_w_out": nrm(ks[18], (DEPTH, FFN_HIDDEN, D), FFN_HIDDEN ** -0.5),
    }

def first_block(x, c, ctx, c_ctx, ada_w, ada_b, norm_g, ab_w_in, ab_w_out, pool_w, pool_scale,
              hg_lower, hg_onorm_g, att_w_in, att_w_out, att_qnorm_g, att_knorm_g, ffn_w_in, ffn_w_out):
    lb_all = jnp.cumsum(jax.nn.softmax(hg_lower.astype(F32), axis=0), axis=0)
    ctx_s = ctx
    for l in range(DEPTH):
        j = l // 2
        need_ctx = l < DEPTH - 1
        m_lat = (jax.nn.silu(c) @ ada_w[l] + ada_b[l])[:, None]
        m_ctx = jax.nn.silu(c_ctx) @ ada_w[l] + ada_b[l]
        sh1, sc1, g1, sh2, sc2, g2 = jnp.split(m_lat, 6, axis=-1)
        csh1, csc1, cg1, csh2, csc2, cg2 = jnp.split(m_ctx, 6, axis=-1)

        h_lat = rmsnorm(x, norm_g[l, 0]) * (1.0 + sc1) + sh1
        h_ctx = rmsnorm(ctx_s, norm_g[l, 0]) * (1.0 + csc1) + csh1
        if l % 2 == 0:
            y_lat, y_ctx = pool_hgrn_mixer(h_lat, h_ctx, ab_w_in[j], ab_w_out[j], pool_w[j], pool_scale[j],
                                           lb_all[j], hg_onorm_g[j], need_ctx)
        else:
            y_lat, y_ctx = gqa_mixer(h_lat, h_ctx, att_w_in[j], att_w_out[j], att_qnorm_g[j], att_knorm_g[j],
                                     need_ctx)
        x = x + g1 * rmsnorm(y_lat, norm_g[l, 1])
        f_lat = swiglu(rmsnorm(x, norm_g[l, 2]) * (1.0 + sc2) + sh2, ffn_w_in[l], ffn_w_out[l])
        x = x + g2 * rmsnorm(f_lat, norm_g[l, 3])

        if need_ctx:
            ctx_s = ctx_s + cg1 * rmsnorm(y_ctx, norm_g[l, 1])
            f_ctx = swiglu(rmsnorm(ctx_s, norm_g[l, 2]) * (1.0 + csc2) + csh2, ffn_w_in[l], ffn_w_out[l])
            ctx_s = ctx_s + cg2 * rmsnorm(f_ctx, norm_g[l, 3])
    return x


CHUNK = 64
D_PLE = 256
N_EVEN_2 = (DEPTH + 1) // 2
N_ODD_2 = DEPTH // 2
D_FF = 2816
A_HEADS = 8
A_KV_HEADS = 2
A_GROUP = A_HEADS // A_KV_HEADS
A_HEAD_DIM = 64
A_WIDTH = A_HEADS * A_HEAD_DIM
A_KV_WIDTH = A_KV_HEADS * A_HEAD_DIM
A_WINDOW = 128
A_PREV_CHUNKS = A_WINDOW // CHUNK
B_WIDTH = 512
B_BLOCKS = 8
B_BLOCK = B_WIDTH // B_BLOCKS
B_CONV = 4
RG_C = 8.0
AB_PROJ = A_WIDTH + 2 * A_KV_WIDTH + 2 * B_WIDTH
C_HEADS = 8
C_HEAD_DIM = 128
C_WIDTH = C_HEADS * C_HEAD_DIM
C_CONV = 4
C_PROJ = 4 * C_WIDTH + 2 * C_HEADS
DN_ALPHA = (2.0 * DEPTH) ** 0.25
DN_BETA = (8.0 * DEPTH) ** -0.25
LN_EPS = 1e-5
NORM_EPS = 1e-6
NEG = -1e30


def layer_norm(x, g, b):
    xf = x.astype(jnp.float32)
    mu = jnp.mean(xf, -1, keepdims=True)
    var = jnp.mean(jnp.square(xf - mu), -1, keepdims=True)
    return ((xf - mu) * lax.rsqrt(var + LN_EPS) * g + b).astype(x.dtype)

def swiglu_2(x, wg, wu, wd):
    return (jax.nn.silu(x @ wg) * (x @ wu)) @ wd

def causal_dwconv(x, w):
    k, s = w.shape[0], x.shape[1]
    xp = jnp.pad(x, ((0, 0), (k - 1, 0), (0, 0)))
    y = xp[:, 0:s] * w[0]
    for j in range(1, k):
        y = y + xp[:, j:j + s] * w[j]
    return y

def chunk_band(t, n_prev):
    b, s = t.shape[:2]
    nc = s // CHUNK
    pad = n_prev * CHUNK
    tp = jnp.pad(t, ((0, 0), (pad, 0), (0, 0), (0, 0)))
    return jnp.concatenate(
        [tp[:, j * CHUNK:j * CHUNK + s].reshape(b, nc, CHUNK, *t.shape[2:]) for j in range(n_prev + 1)],
        axis=2)

def alibi_slopes(n):
    return 2.0 ** (-8.0 * jnp.arange(1, n + 1, dtype=jnp.float32) / n)

def sliding_window_sink_attention(q, k, v, sinks):
    b, s = q.shape[:2]
    nc = s // CHUNK
    pad = A_PREV_CHUNKS * CHUNK
    nk = pad + CHUNK
    qb = q.reshape(b, nc, CHUNK, A_KV_HEADS, A_GROUP, A_HEAD_DIM)
    kb = chunk_band(k, A_PREV_CHUNKS)
    vb = chunk_band(v, A_PREV_CHUNKS)
    sc = jnp.einsum('bnckgd,bnskd->bnkgcs', qb, kb).astype(jnp.float32) * (A_HEAD_DIM ** -0.5)
    dist = jnp.abs(jnp.arange(CHUNK)[:, None] + pad - jnp.arange(nk)[None, :]).astype(jnp.float32)
    slopes = alibi_slopes(A_HEADS).reshape(A_KV_HEADS, A_GROUP)
    valid = (jnp.arange(nc)[:, None] * CHUNK + jnp.arange(nk)[None, :] - pad) >= 0
    sc = sc - slopes[:, :, None, None] * dist
    sc = jnp.where(valid[None, :, None, None, None, :], sc, NEG)
    sink = sinks.astype(jnp.float32).reshape(A_KV_HEADS, A_GROUP)[:, :, None]
    m = jnp.maximum(sc.max(-1), sink)
    pr = jnp.exp(sc - m[..., None])
    den = pr.sum(-1) + jnp.exp(sink - m)
    o = jnp.einsum('bnkgcs,bnskd->bnckgd', pr / den[..., None], vb.astype(jnp.float32))
    return o.reshape(b, s, A_WIDTH).astype(q.dtype)

def rg_lru(x, w_a, b_a, w_x, b_x, lam):
    xb = x.reshape(*x.shape[:2], B_BLOCKS, B_BLOCK)
    r = jax.nn.sigmoid(jnp.einsum('bshi,hij->bshj', xb, w_a).reshape(x.shape) + b_a)
    i = jax.nn.sigmoid(jnp.einsum('bshi,hij->bshj', xb, w_x).reshape(x.shape) + b_x)
    log_a = (-RG_C * r * jax.nn.softplus(-lam)).astype(jnp.float32)
    a = jnp.exp(log_a)
    u = jnp.sqrt(-jnp.expm1(2.0 * log_a)) * (i * x).astype(jnp.float32)

    def combine(c1, c2):
        a1, b1 = c1
        a2, b2 = c2
        return a1 * a2, a2 * b1 + b2

    _, h = lax.associative_scan(combine, (a, u), axis=1)
    return h.astype(x.dtype)

def mixer_ab(x, w_in, sinks, conv_w, conv_b, w_a, b_a, w_x, b_x, lam, w_out):
    b, s = x.shape[:2]
    proj = x @ w_in
    o1 = A_WIDTH
    o2 = o1 + A_KV_WIDTH
    o3 = o2 + A_KV_WIDTH
    o4 = o3 + B_WIDTH
    q = proj[..., :o1].reshape(b, s, A_HEADS, A_HEAD_DIM)
    k = proj[..., o1:o2].reshape(b, s, A_KV_HEADS, A_HEAD_DIM)
    v = proj[..., o2:o3].reshape(b, s, A_KV_HEADS, A_HEAD_DIM)
    bx = proj[..., o3:o4]
    bg = proj[..., o4:]
    ya = sliding_window_sink_attention(q, k, v, sinks)
    bx = causal_dwconv(bx, conv_w) + conv_b
    yb = rg_lru(bx, w_a, b_a, w_x, b_x, lam) * jax.nn.gelu(bg)
    return jnp.concatenate([ya, yb], axis=-1) @ w_out

def gated_delta_rule(q, k, v, g, beta):
    f32 = jnp.float32
    b, s, h, dk = q.shape
    dv = v.shape[-1]
    nc = s // CHUNK

    def to_chunks(t):
        return t.astype(f32).reshape(b, nc, CHUNK, h, -1).transpose(1, 0, 3, 2, 4)

    q = to_chunks(q) * (dk ** -0.5)
    k = to_chunks(k)
    v = to_chunks(v)
    g = g.astype(f32).reshape(b, nc, CHUNK, h).transpose(1, 0, 3, 2)
    beta = beta.astype(f32).reshape(b, nc, CHUNK, h).transpose(1, 0, 3, 2)
    gc = jnp.cumsum(g, axis=-1)
    tril = jnp.tril(jnp.ones((CHUNK, CHUNK), bool))
    strict = jnp.tril(jnp.ones((CHUNK, CHUNK), bool), -1)
    diff = gc[..., :, None] - gc[..., None, :]
    decay = jnp.where(tril, jnp.exp(jnp.where(tril, diff, 0.0)), 0.0)
    kb = k * beta[..., None]
    lmat = jnp.where(strict, jnp.einsum('nbhid,nbhjd->nbhij', kb, k) * decay, 0.0)
    amat = lmat + jnp.eye(CHUNK, dtype=f32)
    u = lax.linalg.triangular_solve(amat, v * beta[..., None], left_side=True, lower=True, unit_diagonal=True)
    w = lax.linalg.triangular_solve(amat, kb * jnp.exp(gc)[..., None], left_side=True, lower=True, unit_diagonal=True)
    attn = jnp.einsum('nbhid,nbhjd->nbhij', q, k) * decay
    qg = q * jnp.exp(gc)[..., None]
    kdec = k * jnp.exp(gc[..., -1:] - gc)[..., None]
    glast = jnp.exp(gc[..., -1])

    def step(state, xs):
        qg_n, kdec_n, w_n, u_n, attn_n, gl_n = xs
        v_new = u_n - jnp.einsum('bhcd,bhde->bhce', w_n, state)
        o = jnp.einsum('bhcd,bhde->bhce', qg_n, state) + jnp.einsum('bhij,bhje->bhie', attn_n, v_new)
        state = state * gl_n[..., None, None] + jnp.einsum('bhcd,bhce->bhde', kdec_n, v_new)
        return state, o

    s0 = jnp.zeros((b, h, dk, dv), f32)
    _, o = lax.scan(step, s0, (qg, kdec, w, u, attn, glast))
    return o.transpose(1, 0, 3, 2, 4).reshape(b, s, h, dv)

def mixer_c(x, w_in, conv_w, a_log, dt_bias, norm_g, w_out):
    b, s = x.shape[:2]
    proj = x @ w_in
    qkv = jax.nn.silu(causal_dwconv(proj[..., :3 * C_WIDTH], conv_w))
    z = proj[..., 3 * C_WIDTH:4 * C_WIDTH].reshape(b, s, C_HEADS, C_HEAD_DIM)
    b_logit = proj[..., 4 * C_WIDTH:4 * C_WIDTH + C_HEADS]
    a_in = proj[..., 4 * C_WIDTH + C_HEADS:]
    q = qkv[..., :C_WIDTH].reshape(b, s, C_HEADS, C_HEAD_DIM).astype(jnp.float32)
    k = qkv[..., C_WIDTH:2 * C_WIDTH].reshape(b, s, C_HEADS, C_HEAD_DIM).astype(jnp.float32)
    v = qkv[..., 2 * C_WIDTH:].reshape(b, s, C_HEADS, C_HEAD_DIM)
    q = q * lax.rsqrt(jnp.sum(q * q, -1, keepdims=True) + NORM_EPS)
    k = k * lax.rsqrt(jnp.sum(k * k, -1, keepdims=True) + NORM_EPS)
    beta = jax.nn.sigmoid(b_logit.astype(jnp.float32))
    g = -jnp.exp(a_log.astype(jnp.float32)) * jax.nn.softplus((a_in + dt_bias).astype(jnp.float32))
    o = gated_delta_rule(q, k, v, g, beta)
    o = o * lax.rsqrt(jnp.mean(o * o, -1, keepdims=True) + NORM_EPS) * norm_g
    o = (o * jax.nn.silu(z.astype(jnp.float32))).astype(x.dtype)
    return o.reshape(b, s, C_WIDTH) @ w_out

def second_inputs(seed: int = 0) -> dict:
    key = jax.random.key(seed)
    ks = iter(jax.random.split(key, 48))
    f32 = jnp.float32

    def nrm(shape, scale):
        return jax.random.normal(next(ks), shape, f32) * scale

    d = D_MODEL
    x = nrm((BATCH, SEQ, d), 1.0)
    p = nrm((DEPTH, BATCH, SEQ, D_PLE), 1.0)
    ffn1_wg = nrm((DEPTH, d, D_FF), d ** -0.5)
    ffn1_wu = nrm((DEPTH, d, D_FF), d ** -0.5)
    ffn1_wd = nrm((DEPTH, D_FF, d), DN_BETA * D_FF ** -0.5)
    ffn2_wg = nrm((DEPTH, d, D_FF), d ** -0.5)
    ffn2_wu = nrm((DEPTH, d, D_FF), d ** -0.5)
    ffn2_wd = nrm((DEPTH, D_FF, d), DN_BETA * D_FF ** -0.5)
    ln_g = 1.0 + nrm((DEPTH, 3, d), 0.02)
    ln_b = nrm((DEPTH, 3, d), 0.02)
    ple_wg = nrm((DEPTH, d, d), d ** -0.5)
    ple_bg = nrm((DEPTH, d), 0.02)
    ple_wp = nrm((DEPTH, D_PLE, d), D_PLE ** -0.5)
    ab_w_in = nrm((N_EVEN_2, d, AB_PROJ), d ** -0.5)
    a_sinks = nrm((N_EVEN_2, A_HEADS), 0.5)
    b_conv_w = nrm((N_EVEN_2, B_CONV, B_WIDTH), B_CONV ** -0.5)
    b_conv_b = nrm((N_EVEN_2, B_WIDTH), 0.02)
    b_wa = nrm((N_EVEN_2, B_BLOCKS, B_BLOCK, B_BLOCK), B_BLOCK ** -0.5)
    b_ba = nrm((N_EVEN_2, B_WIDTH), 0.02)
    b_wx = nrm((N_EVEN_2, B_BLOCKS, B_BLOCK, B_BLOCK), B_BLOCK ** -0.5)
    b_bx = nrm((N_EVEN_2, B_WIDTH), 0.02)
    a_c = jax.random.uniform(next(ks), (N_EVEN_2, B_WIDTH), f32, 0.9, 0.999)
    a0 = a_c ** (1.0 / RG_C)
    b_lam = jnp.log(a0) - jnp.log1p(-a0)
    ab_w_out = nrm((N_EVEN_2, A_WIDTH + B_WIDTH, d), DN_BETA * (A_WIDTH + B_WIDTH) ** -0.5)
    c_w_in = nrm((N_ODD_2, d, C_PROJ), d ** -0.5)
    c_conv_w = nrm((N_ODD_2, C_CONV, 3 * C_WIDTH), C_CONV ** -0.5)
    c_a_log = jnp.log(jax.random.uniform(next(ks), (N_ODD_2, C_HEADS), f32, 1.0, 16.0))
    dt = jnp.exp(jax.random.uniform(next(ks), (N_ODD_2, C_HEADS), f32, np.log(1e-3), np.log(1e-1)))
    c_dt_bias = dt + jnp.log(-jnp.expm1(-dt))
    c_norm_g = 1.0 + nrm((N_ODD_2, C_HEAD_DIM), 0.02)
    c_w_out = nrm((N_ODD_2, C_WIDTH, d), DN_BETA * C_WIDTH ** -0.5)
    return {'x': x, 'p': p,
            'ffn1_wg': ffn1_wg, 'ffn1_wu': ffn1_wu, 'ffn1_wd': ffn1_wd,
            'ffn2_wg': ffn2_wg, 'ffn2_wu': ffn2_wu, 'ffn2_wd': ffn2_wd,
            'ln_g': ln_g, 'ln_b': ln_b,
            'ple_wg': ple_wg, 'ple_bg': ple_bg, 'ple_wp': ple_wp,
            'ab_w_in': ab_w_in, 'a_sinks': a_sinks,
            'b_conv_w': b_conv_w, 'b_conv_b': b_conv_b,
            'b_wa': b_wa, 'b_ba': b_ba, 'b_wx': b_wx, 'b_bx': b_bx, 'b_lam': b_lam,
            'ab_w_out': ab_w_out,
            'c_w_in': c_w_in, 'c_conv_w': c_conv_w, 'c_a_log': c_a_log, 'c_dt_bias': c_dt_bias,
            'c_norm_g': c_norm_g, 'c_w_out': c_w_out}

def second_block(x, p, ffn1_wg, ffn1_wu, ffn1_wd, ffn2_wg, ffn2_wu, ffn2_wd, ln_g, ln_b,
              ple_wg, ple_bg, ple_wp, ab_w_in, a_sinks, b_conv_w, b_conv_b,
              b_wa, b_ba, b_wx, b_bx, b_lam, ab_w_out,
              c_w_in, c_conv_w, c_a_log, c_dt_bias, c_norm_g, c_w_out):
    for i in range(DEPTH):
        j = i // 2
        x = layer_norm(DN_ALPHA * x + 0.5 * swiglu_2(x, ffn1_wg[i], ffn1_wu[i], ffn1_wd[i]), ln_g[i, 0], ln_b[i, 0])
        if i % 2 == 0:
            y = mixer_ab(x, ab_w_in[j], a_sinks[j], b_conv_w[j], b_conv_b[j],
                         b_wa[j], b_ba[j], b_wx[j], b_bx[j], b_lam[j], ab_w_out[j])
        else:
            y = mixer_c(x, c_w_in[j], c_conv_w[j], c_a_log[j], c_dt_bias[j], c_norm_g[j], c_w_out[j])
        x = layer_norm(DN_ALPHA * x + y, ln_g[i, 1], ln_b[i, 1])
        x = layer_norm(DN_ALPHA * x + 0.5 * swiglu_2(x, ffn2_wg[i], ffn2_wu[i], ffn2_wd[i]), ln_g[i, 2], ln_b[i, 2])
        x = x + jax.nn.sigmoid(x @ ple_wg[i] + ple_bg[i]) * (p[i] @ ple_wp[i])
    return x


def setup_inputs(seed=0):
    out = dict(first_inputs(seed))
    for name, value in second_inputs(seed + 1).items():
        if name != "x":
            out[name + "_2"] = value
    return out


def reference(
    x, c, ctx, c_ctx, ada_w, ada_b, norm_g, ab_w_in, ab_w_out, pool_w, pool_scale, hg_lower,
    hg_onorm_g, att_w_in, att_w_out, att_qnorm_g, att_knorm_g, ffn_w_in, ffn_w_out, p_2,
    ffn1_wg_2, ffn1_wu_2, ffn1_wd_2, ffn2_wg_2, ffn2_wu_2, ffn2_wd_2, ln_g_2, ln_b_2, ple_wg_2,
    ple_bg_2, ple_wp_2, ab_w_in_2, a_sinks_2, b_conv_w_2, b_conv_b_2, b_wa_2, b_ba_2, b_wx_2,
    b_bx_2, b_lam_2, ab_w_out_2, c_w_in_2, c_conv_w_2, c_a_log_2, c_dt_bias_2, c_norm_g_2,
    c_w_out_2,
):
    x = first_block(
        x, c, ctx, c_ctx, ada_w, ada_b, norm_g, ab_w_in, ab_w_out, pool_w, pool_scale, hg_lower,
        hg_onorm_g, att_w_in, att_w_out, att_qnorm_g, att_knorm_g, ffn_w_in, ffn_w_out,
    )
    return second_block(
        x, p_2, ffn1_wg_2, ffn1_wu_2, ffn1_wd_2, ffn2_wg_2, ffn2_wu_2, ffn2_wd_2, ln_g_2,
        ln_b_2, ple_wg_2, ple_bg_2, ple_wp_2, ab_w_in_2, a_sinks_2, b_conv_w_2, b_conv_b_2,
        b_wa_2, b_ba_2, b_wx_2, b_bx_2, b_lam_2, ab_w_out_2, c_w_in_2, c_conv_w_2, c_a_log_2,
        c_dt_bias_2, c_norm_g_2, c_w_out_2,
    )


_drawn_inputs = setup_inputs


def setup_inputs(seed=0):
    import zlib

    import numpy as np

    out = dict(_drawn_inputs(seed))
    spreads = {}
    factors = {'norm_g': 3.676,
     'hg_lower': 8.0,
     'hg_onorm_g': 8.0,
     'att_qnorm_g': 8.0,
     'att_knorm_g': 8.0,
     'ple_bg_2': 8.0,
     'a_sinks_2': 8.0,
     'b_conv_b_2': 4.898,
     'b_ba_2': 64.0,
     'b_bx_2': 45.448,
     'c_norm_g_2': 25.493}
    for name, (base, spread) in spreads.items():
        noise = np.random.default_rng([zlib.crc32(name.encode()), seed]).standard_normal(out[name].shape)
        drawn = base * np.exp(spread * noise) if base else spread * noise
        out[name] = jnp.asarray(drawn.astype(out[name].dtype))
    for name, factor in factors.items():
        out[name] = (out[name] * factor).astype(out[name].dtype)
    return out
```

```python
from contextlib import ExitStack

import numpy as np

import concourse.bass as bass
from concourse import mybir

F32 = mybir.dt.float32
F32R = mybir.dt.float32r
U8 = mybir.dt.uint8
ALU = mybir.AluOpType
ACT = mybir.ActivationFunctionType
AX = mybir.AxisListType

P = 128
D = 1024
DT = D // P
T = 256
T2 = 2 * T
CTX, LAT, BOTH = slice(0, T), slice(T, T2), slice(0, T2)
CHUNK_COLS = 2048
SLOTS = 6
FF = 2816
FF_STEPS = FF // 256
FF_CHUNKS = 3 * FF_STEPS
RMS_EPS = 1e-6
LN_EPS = 1e-5
ALPHA2 = 2.0
ALPHA = ALPHA2 ** 0.5
HEADS = 4
LEVELS = 7
NCH = T2 // P

STAGES = [("ada0", 24), ("mix0_in", 12), ("mix0_out", 4), ("ffn0_lat", FF_CHUNKS), ("ffn0_ctx", FF_CHUNKS),
          ("ada1", 24), ("mix1_in", 6), ("mix1_out", 4), ("ffn1_lat", FF_CHUNKS),
          ("ffn2", FF_CHUNKS), ("mix2_in", 7), ("mix2_out", 4), ("ffn3", FF_CHUNKS), ("ple2", 5),
          ("ffn4", FF_CHUNKS), ("mix3_in", 16), ("mix3_out", 4), ("ffn5", FF_CHUNKS), ("ple3", 5)]
START, _n = {}, 0
for _name, _count in STAGES:
    START[_name] = _n
    _n += _count
N_USES = _n
N_CHUNKS = N_USES - FF_CHUNKS

SMALL = {}
_at = 0
for _name, _width in [("cvec", 16), ("ada_b", 96), ("norm_g", 64), ("lower", 16), ("pool_scale", 4),
                      ("onorm", 1), ("qnorm", 1), ("knorm", 1), ("ln_g", 48), ("ln_b", 48),
                      ("ple_bg", 16), ("conv_b", 4), ("b_ba", 4), ("b_bx", 4), ("b_lam", 4),
                      ("b_conv", 16), ("c_conv", 96), ("c_norm", 1), ("sinks", 8), ("a_log", 1),
                      ("dt_bias", 1), ("w_ba", 128), ("pool_w", 512)]:
    SMALL[_name] = slice(_at, _at + _width)
    _at += _width
SMALL_COLS = _at

G_MIX, SH_MIX, G_MIXOUT, G_FFN, SH_FFN, G_FFNOUT = range(6)


class Signals:

    def __init__(self, nc, stack, counts):
        self.nc, self.stack, self.counts = nc, stack, counts
        self.sems, self.raised, self.marks = {}, {}, {}

    def __getitem__(self, name):
        if name not in self.sems:
            self.sems[name] = self.stack.enter_context(self.nc.semaphore(name))
        return self.sems[name]

    def mark(self, name, key=None, by=1):
        self.raised[name] = self.raised.get(name, 0) + by
        self.marks[name, key] = self.raised[name]
        return by

    def at(self, name, key=None):
        return 1 if self.counts is None else self.counts[name, key]


class Order:

    def __init__(self, sem):
        self.sem, self.n = sem, 0

    def step(self):
        self.n += 1
        return 1


def bc(ap, shape):
    return ap.broadcast_to(shape)


def build(nc, stream, small, xt, consts, masks, extra, out, counts=None, stop=None, dbg=None):
    with ExitStack() as stack:
        sb = lambda name, shape, dt=F32: stack.enter_context(nc.sbuf_tensor(name, shape, dt))
        S = Signals(nc, stack, counts)
        ARENA_COLS = 24832

        def same_place(name, shape):
            with nc.sbuf_tensor(name, shape, F32R) as rounded:
                return rounded

        RING_R = same_place("ring_r", [P, SLOTS, CHUNK_COLS])
        ring = sb("ring", [P, SLOTS, CHUNK_COLS])
        AR_R = same_place("AR_r", [P, ARENA_COLS])
        AR = sb("AR", [P, ARENA_COLS])
        X = sb("X", [P, DT, T2])
        H = sb("H", [P, DT, T2])
        SQ = sb("SQ", [P, DT, T2])
        RI = sb("RI", [P, T2])
        SM = sb("SM", [P, SMALL_COLS])
        CO = sb("CO", [P, 4 * P])
        M8 = sb("M8", [P, 2 * LEVELS * 256], U8)
        CS = sb("CS", [P, DT, 2])
        MOD = sb("MOD", [P, 48, 2])
        GV = sb("GV", [P, 6, DT, 2])
        EPS = sb("EPS", [P, 3])
        TMP = sb("TMP", [P, 64])
        ZERO = sb("ZERO", [P, P])
        PS = stack.enter_context(nc.psum_tensor("PS", [P, 8, 512], F32))
        IDENT, ONES, ROPE, CAUSAL = (CO[:, i * P:(i + 1) * P] for i in range(4))
        sm = lambda name: SM[:, SMALL[name]]
        mod_of = lambda kind, k, s: GV[:, kind, k, s:s + 1]
        STREAM = {0: LAT, 1: CTX}

        arrived = [S[f"chunk_arrived_{i}"] for i in range(SLOTS)]
        multiplied = S["chunk_multiplied"]
        ffn_silu = S["ffn_silu"]
        ffn_hidden = S["ffn_hidden"]
        ffn_gated = S["ffn_gated"]
        split_hi = S["split_hi"]
        split_lo = S["split_lo"]
        FFN_INDEX = {n: i for i, n in enumerate(k for k, _ in STAGES if k.startswith("ffn"))}

        def arena(at, *shape, of=AR):
            n = int(np.prod(shape))
            assert at + n <= ARENA_COLS
            v = of[:, at:at + n]
            if len(shape) == 1:
                return v
            names = "abcd"[:len(shape)]
            return v.rearrange(f"p ({' '.join(names)}) -> p {' '.join(names)}",
                               **{c: s for c, s in zip(names, shape)})

        MASKS = H.rearrange("p a b -> p (a b)")[:, 0:2 * LEVELS * 256]
        GATE = arena(22784, 2, 512)
        HIDDEN = arena(23808, 2, 2 * T)
        W_HI = arena(8192, 3, CHUNK_COLS, of=AR_R)
        X_HI, X_LO = (arena(14336 + 2048 * i, DT, T, of=AR_R) for i in range(2))
        G_HI, G_LO = (arena(18432 + 1024 * i, 2, 2, T, of=AR_R) for i in range(2))

        def need_chunk(eng, n):
            eng.wait_ge(arrived[n % SLOTS], 16 * (n // SLOTS + 1))

        def need_product(eng, n):
            eng.wait_ge(multiplied, n + 1)

        def pe_chunk_tokens_move(pe, n, x, cols, bank, width):
            need_chunk(pe, n)
            for j in range(2):
                o = PS[:, bank + j, 0:width] if width == T2 else PS[:, bank, j * T:(j + 1) * T]
                for k in range(DT):
                    ins = pe.matmul(o, ring[:, n % SLOTS, k * 256 + j * P:k * 256 + (j + 1) * P],
                                    x[:, k, cols], start=(k == 0), stop=(k == DT - 1))
            ins.then_inc(multiplied, 1)

        def pe_chunk_tokens_stay(pe, n, x, first, tiles, bank):
            need_chunk(pe, n)
            for t in range(tiles):
                for k in range(DT):
                    ins = pe.matmul(PS[:, bank + t // 2, (t % 2) * 256:(t % 2 + 1) * 256],
                                    x[:, k, first + t * P:first + (t + 1) * P],
                                    ring[:, n % SLOTS, k * 256:(k + 1) * 256],
                                    start=(k == 0), stop=(k == DT - 1))
            ins.then_inc(multiplied, 1)

        def pe_sum_features(pe, tag, src, width, bank=7):
            for k, a in enumerate(src):
                ins = pe.matmul(PS[:, bank, 0:width], ONES, a, start=(k == 0), stop=(k == len(src) - 1))
            ins.then_inc(S["feature_sums"], S.mark("feature_sums", tag))

        def pe_norm(pe, tag, cols):
            pe.wait_ge(S["squares"], S.at("squares", tag))
            pe_sum_features(pe, tag, [SQ[:, k, cols] for k in range(DT)], cols.stop - cols.start)

        def pe_ada(pe, layer):
            n0 = START[f"ada{layer}"]
            with pe.Fori(0, 24 // SLOTS) as r:
                for j in range(SLOTS):
                    pe.wait_ge(arrived[(n0 + j) % SLOTS], r * 16 + 16 * ((n0 + j) // SLOTS + 1))
                    for i in range(2):
                        for k in range(DT):
                            w = ring[:, (n0 + j) % SLOTS, k * 256 + i * P:k * 256 + (i + 1) * P]
                            ins = pe.matmul(PS[:, 6, bass.ds(r * (4 * SLOTS) + (4 * j + 2 * i), 2)], w, CS[:, k, :],
                                            start=(k == 0), stop=(k == DT - 1), skip_group_check=True)
                    ins.then_inc(multiplied, 1)

        def pe_ffn(pe, tag):
            n0, c = START[tag], FFN_INDEX[tag]
            g0, s0 = c * FF_STEPS, c * FF_CHUNKS

            def need_split(r, i):
                pe.wait_ge(split_lo, r + (s0 + i + 1))

            def gate_up(d, i, r):
                for half in range(2):
                    n = n0 + i + half
                    need_split(r, i + half)
                    for j in range(2):
                        o = PS[:, 4 + 2 * d + half, j * T:(j + 1) * T]
                        for k in range(DT):
                            if i + half + j == 0 and k == 4:
                                pe.wait_ge(S["x_lo"], S.at("x_lo", (tag, 1)))
                            w = slice(k * 256 + j * P, k * 256 + (j + 1) * P)
                            w_hi, w_lo = W_HI[:, (i + half) % 3, w], RING_R[:, n % SLOTS, w]
                            pe.matmul(o, w_hi, X_HI[:, k, :], start=(k == 0), stop=False)
                            pe.matmul(o, w_hi, X_LO[:, k, :], start=False, stop=False)
                            ins = pe.matmul(o, w_lo, X_HI[:, k, :], start=False, stop=(k == DT - 1))
                    ins.then_inc(multiplied, 1)

            def down(d, i, last, r):
                n = n0 + i
                need_split(r, i)
                for f in range(2):
                    for m in range(DT):
                        o = PS[:, m // 2, (m % 2) * T:(m % 2 + 1) * T]
                        w = slice(f * D + m * P, f * D + (m + 1) * P)
                        w_hi, w_lo = W_HI[:, i % 3, w], RING_R[:, n % SLOTS, w]
                        pe.matmul(o, w_hi, G_HI[:, d, f, :], start=False, stop=False, skip_group_check=True)
                        pe.matmul(o, w_hi, G_LO[:, d, f, :], start=False, stop=False, skip_group_check=True)
                        ins = pe.matmul(o, w_lo, G_HI[:, d, f, :], start=False, stop=(last and f == 1), skip_group_check=True)
                ins.then_inc(multiplied, 1)

            pe.wait_ge(S["x_lo"], S.at("x_lo", (tag, 0)))
            for b in range(4):
                pe.matmul(PS[:, b, 0:2], ZERO[:, :], ZERO[:, 0:2], start=True, stop=False, skip_group_check=True)
            gate_up(0, 0, 0)
            with pe.Fori(0, (FF_STEPS - 1) // 2) as r:
                for it in (1, 2):
                    gate_up(it % 2, 3 * it - 1, r * 6)
                    pe.wait_ge(ffn_gated, r * 2 + (g0 + it))
                    down((it - 1) % 2, 3 * it + 1, False, r * 6)
            pe.wait_ge(ffn_gated, g0 + FF_STEPS)
            down((FF_STEPS - 1) % 2, FF_CHUNKS - 1, True, 0)

        def sp_load(sp, n, i, wait, slot):
            if wait is not None:
                sp.wait_ge(multiplied, wait)
            src = stream[bass.ds(i, 1), :, :].rearrange("o p n -> p (o n)")
            sp.dma_start(ring[:, slot, :], src).then_inc(arrived[slot], 16)

        def sp_stream(sp, first, count, shift):
            n = first
            while n < first + count and (n < SLOTS or (first + count - n) % SLOTS or n % SLOTS):
                sp_load(sp, n, n - shift, n + 1 - SLOTS if n >= SLOTS else None, n % SLOTS)
                n += 1
            rounds = (first + count - n) // SLOTS
            if rounds:
                with sp.Fori(0, rounds) as r:
                    for j in range(SLOTS):
                        sp_load(sp, n + j, r * SLOTS + (n + j - shift), r * SLOTS + (n + j + 1 - SLOTS), j)

        def act_rinv(act, order, tag, width, of, eps, bank=7):
            act.wait_ge(S["feature_sums"], S.at("feature_sums", tag))
            act.activation(RI[:, 0:width], PS[:, bank, 0:width], ACT.Ln, scale=1.0 / of, bias=EPS[:, eps:eps + 1]).then_inc(order.sem, order.step())
            act.wait_ge(order.sem, order.n)
            act.activation(RI[:, 0:width], RI[:, 0:width], ACT.Exp, scale=-0.5).then_inc(S["rinv"], S.mark("rinv", tag))

        def act_squares(act, tag, src, cols):
            act.activation(SQ[:, :, cols], src, ACT.Square).then_inc(S["squares"], S.mark("squares", tag))

        def act_split_chunk(act, tag, i, r=0, turns=0):
            n = START[tag] + i
            act.wait_ge(arrived[n % SLOTS], turns * 16 + 16 * (n // SLOTS + 1))
            act.wait_ge(multiplied, r + (START[tag] + max(i - 2, 0)))
            act.activation(W_HI[:, i % 3, :], ring[:, n % SLOTS, :], ACT.Identity).then_inc(split_hi, 1)

        def dve_split_chunk(dve, tag, i, r=0):
            n = START[tag] + i
            dve.wait_ge(split_hi, r + (FFN_INDEX[tag] * FF_CHUNKS + i + 1))
            dve.tensor_tensor(RING_R[:, n % SLOTS, :], ring[:, n % SLOTS, :], W_HI[:, i % 3, :], ALU.subtract).then_inc(split_lo, 1)

        def act_split_first(act, tag):
            for i in range(3):
                act_split_chunk(act, tag, i)

        def dve_split_first(dve, tag):
            for i in range(3):
                dve_split_chunk(dve, tag, i)

        def act_split_input(act, tag, x):
            act.wait_ge(multiplied, START[tag])
            for h in range(2):
                act.activation(X_HI[:, 4 * h:4 * h + 4, :], x[:, 4 * h:4 * h + 4, :], ACT.Identity).then_inc(S["x_hi"], S.mark("x_hi", (tag, h)))

        def dve_split_input(dve, tag, x):
            for h in range(2):
                dve.wait_ge(S["x_hi"], S.at("x_hi", (tag, h)))
                dve.tensor_tensor(X_LO[:, 4 * h:4 * h + 4, :], x[:, 4 * h:4 * h + 4, :], X_HI[:, 4 * h:4 * h + 4, :],
                                  ALU.subtract).then_inc(S["x_lo"], S.mark("x_lo", (tag, h)))

        def act_ffn(act, tag):
            n0 = START[tag]

            def silu(it, r=0):
                act.wait_ge(multiplied, r + (n0 + max(3 * it - 1, 0) + 1))
                act.activation(GATE[:, it % 2, :], PS[:, 4 + 2 * (it % 2), :], ACT.Silu).then_inc(ffn_silu, 1)

            def splits(it, r=0, turns=0):
                for i in range(3 * it + (2 if it else 3), min(3 * it + 5, FF_CHUNKS)):
                    act_split_chunk(act, tag, i, r, turns)

            silu(0)
            splits(0)
            with act.Fori(0, (FF_STEPS - 3) // 2) as r:
                for it in (1, 2):
                    silu(it, r * 6)
                    splits(it, r * 6, r)
            for it in (FF_STEPS - 2, FF_STEPS - 1):
                silu(it)
                splits(it)

        def dve_ffn(dve, tag):
            n0, g0 = START[tag], FFN_INDEX[tag] * FF_STEPS

            def gating(it, steps=0, r=0):
                d = it % 2
                dve.wait_ge(ffn_silu, steps + (g0 + it + 1))
                dve.wait_ge(multiplied, r + (n0 + (3 * it if it else 1) + 1))
                if it >= 2:
                    dve.wait_ge(multiplied, r + (n0 + 3 * it - 1))
                gate, up = GATE[:, d, :], PS[:, 5 + 2 * d, :]
                both = lambda ap: ap[:, d, :, :].rearrange("p a b -> p (a b)")
                dve.tensor_tensor(both(G_HI), gate, up, ALU.mult).then_inc(ffn_hidden, 1)
                dve.tensor_tensor(HIDDEN[:, d, :], gate, up, ALU.mult).then_inc(ffn_hidden, 1)
                dve.wait_ge(ffn_hidden, steps * 2 + 2 * (g0 + it + 1))
                dve.tensor_tensor(both(G_LO), HIDDEN[:, d, :], both(G_HI), ALU.subtract).then_inc(ffn_gated, 1)

            gating(0)
            for i in (3, 4):
                dve_split_chunk(dve, tag, i)

            def step(it, steps=0, r=0):
                dve_split_chunk(dve, tag, 3 * it + 2, r)
                gating(it, steps, r)
                for i in range(3 * it + 3, min(3 * it + 5, FF_CHUNKS)):
                    dve_split_chunk(dve, tag, i, r)

            step(1)
            with dve.Fori(0, (FF_STEPS - 3) // 2) as r:
                for it in (2, 3):
                    step(it, r * 2, r * 6)
            step(FF_STEPS - 1)

        def rows(lo, hi):
            return bc(RI[:, lo:hi].unsqueeze(1), [P, DT, hi - lo])

        def dve_modulate(dve, order, tag, cols, g, sh, streams):
            dve.wait_ge(S["rinv"], S.at("rinv", tag))
            dve.tensor_tensor(SQ[:, :, cols], X[:, :, cols], rows(0, cols.stop - cols.start), ALU.mult).then_inc(order.sem, order.step())
            dve.wait_ge(order.sem, order.n)
            for s in streams:
                c = STREAM[s]
                for k in range(DT):
                    ins = dve.tensor_scalar(H[:, k, c], SQ[:, k, c], mod_of(g, k, s), mod_of(sh, k, s), ALU.mult, ALU.add)
                    if s != streams[-1] or k != DT - 1:
                        ins.then_inc(order.sem, order.step())
            ins.then_inc(S["normed"], S.mark("normed", tag))

        def dve_residual(dve, order, tag, y, g, s, ri=0):
            c = STREAM[s]
            dve.wait_ge(S["rinv"], S.at("rinv", tag))
            dve.tensor_tensor(SQ[:, :, c], y, rows(ri, ri + T), ALU.mult).then_inc(order.sem, order.step())
            dve.wait_ge(order.sem, order.n)
            for k in range(DT):
                ins = dve.scalar_tensor_tensor(out=X[:, k, c], in0=SQ[:, k, c], scalar=mod_of(g, k, s), in1=X[:, k, c],
                                               op0=ALU.mult, op1=ALU.add)
                if k < DT - 1:
                    ins.then_inc(order.sem, order.step())
            ins.then_inc(S["residual"], S.mark("residual", (tag, s)))

        def dve_modulation(dve, order, layer):
            need_product(dve, START[f"ada{layer}"] + 23)
            ab = sm("ada_b")[:, layer * 48:(layer + 1) * 48].unsqueeze(2)
            dve.tensor_tensor(MOD[:, :, :], PS[:, 6, 0:96].rearrange("p (a b) -> p a b", b=2),
                                        bc(ab, [P, 48, 2]), ALU.add).then_inc(order.sem, order.step())
            dve.wait_ge(order.sem, order.n)
            ng = lambda i: bc(sm("norm_g")[:, layer * 32 + i * 8:layer * 32 + (i + 1) * 8].unsqueeze(2), [P, DT, 2])
            part = lambda i: MOD[:, i * 8:(i + 1) * 8, :]
            dve.scalar_tensor_tensor(out=GV[:, G_MIX], in0=part(1), scalar=1.0, in1=ng(0), op0=ALU.add, op1=ALU.mult).then_inc(order.sem, order.step())
            dve.tensor_copy(GV[:, SH_MIX], part(0)).then_inc(order.sem, order.step())
            dve.tensor_tensor(GV[:, G_MIXOUT], part(2), ng(1), ALU.mult).then_inc(order.sem, order.step())
            dve.scalar_tensor_tensor(out=GV[:, G_FFN], in0=part(4), scalar=1.0, in1=ng(2), op0=ALU.add, op1=ALU.mult).then_inc(order.sem, order.step())
            dve.tensor_copy(GV[:, SH_FFN], part(3)).then_inc(order.sem, order.step())
            dve.tensor_tensor(GV[:, G_FFNOUT], part(5), ng(3), ALU.mult).then_inc(order.sem, order.step())
            dve.wait_ge(order.sem, order.n)

        Q = arena(0, HEADS, T2)
        GS = arena(2048, HEADS, T2)
        CAT0 = arena(0, DT, T2)
        K2 = arena(4096, 2, HEADS * T2)
        B2 = arena(8192, 2, HEADS * T2)
        V = arena(12288, NCH, 512)
        A = arena(14336, HEADS, T2)
        U = arena(16384, HEADS, 2, T + 32)
        KT = arena(16384 + 2304, 2, 3, 512)
        ST = arena(16384 + 2304 + 3072, 2, 3, 512)
        INVC = arena(16384 + 2304, 4, T)
        SA = arena(16384 + 2304 + 1024, 2, T + 32)
        SB = arena(16384 + 2304 + 1024 + 576, 2, T + 32)
        E2 = SQ[:, :, :].rearrange("p (s a) n -> p s (a n)", s=2)
        W2 = H[:, :, :].rearrange("p (s a) n -> p s (a n)", s=2)
        STEPS = [(lv, d) for lv in range(LEVELS) for d in range(2)]
        ORD = [[0, 1, 2, 3], [1, 0, 3, 2]]

        def halves(ap, lv, which):
            return ap.rearrange("p (n two h) -> p n two h", two=2, h=1 << lv)[:, :, which, :]

        def pe_mix0(pe):
            n0 = START["mix0_in"]
            pe.wait_ge(S["normed"], S.at("normed", "mix0"))
            for i in range(12):
                n, bank = n0 + i, 2 * (i % 3)
                if i >= 3:
                    pe.wait_ge(S[evac0(i - 3)[0]], S.at(*evac0(i - 3)))
                if i in (8, 9):
                    pe_chunk_tokens_stay(pe, n, H, 0, NCH, bank)
                else:
                    pe_chunk_tokens_move(pe, n, H, BOTH, bank, T2)
            pe.wait_ge(S["taken_vector"], S.at("taken_vector", 11))
            pe.wait_ge(S["k_sum"], S.at("k_sum"))
            for h in range(HEADS):
                for c in range(NCH):
                    ins = pe.matmul(PS[:, h, c * P:(c + 1) * P], SQ[:, h, c * P:(c + 1) * P],
                                    Q[:, h, c * P:(c + 1) * P], start=True, stop=True)
            ins.then_inc(S["diag"], S.mark("diag"))
            for i, (lv, d) in enumerate(STEPS):
                pe.wait_ge(S["level_operands"], S.at("level_operands", i))
                if i >= 2:
                    pe.wait_ge(S["level_taken"], S.at("level_taken", i - 2))
                for h in range(HEADS):
                    for c in range(NCH):
                        o = h * T2 + c * P
                        w = W2[:, i % 2, o:o + P]
                        ins = pe.matmul(PS[:, 4 + 2 * (i % 2) + h // 2, (h % 2) * 256 + c * 64:(h % 2) * 256 + (c + 1) * 64],
                                        w, halves(w, lv, 1 - d), start=True, stop=True)
                ins.then_inc(S["level_products"], S.mark("level_products", i))
            for d in range(2):
                for j in range(3):
                    pe.wait_ge(S["khat"], S.at("khat", d))
                    if d * 3 + j >= 4:
                        pe.wait_ge(S["kt"], S.at("kt", (0, d * 3 + j - 4)))
                    for h in range(HEADS):
                        ins = pe.transpose(PS[:, d * 3 + j if d * 3 + j < 4 else d * 3 + j - 4, h * P:(h + 1) * P],
                                           E2[:, d, h * T2 + ORD[d][j] * P:h * T2 + (ORD[d][j] + 1) * P], IDENT)
                    ins.then_inc(S["kt_ready"], S.mark("kt_ready", (d, j)))
            for d in range(2):
                for j in range(3):
                    pe.wait_ge(S["kt"], S.at("kt", (d, j)))
                    if d:
                        pe.wait_ge(S["state"], S.at("state", (d - 1, j)))
                    for h in range(HEADS):
                        ins = pe.matmul(PS[:, 4 + j, h * P:(h + 1) * P], KT[:, d, j, h * P:(h + 1) * P],
                                        V[:, ORD[d][j], h * P:(h + 1) * P], start=True, stop=True)
                    ins.then_inc(S["increment"], S.mark("increment", (d, j)))
            pe.wait_ge(S["qhat"], S.at("qhat"))
            pe.wait_ge(S["state"], S.at("state", (1, 2)))
            for h in range(HEADS):
                for c in range(NCH):
                    o = PS[:, h, c * P:(c + 1) * P]
                    terms = [(V[:, c, h * P:(h + 1) * P], A[:, h, c * P:(c + 1) * P])]
                    for d in range(2):
                        j = ORD[d].index(c)
                        if j:
                            terms.append((ST[:, d, j - 1, h * P:(h + 1) * P], W2[:, d, h * T2 + c * P:h * T2 + (c + 1) * P]))
                    for i, (a, b) in enumerate(terms):
                        ins = pe.matmul(o, a, b, start=(i == 0), stop=(i == len(terms) - 1))
                ins.then_inc(S["mixed"], S.mark("mixed", h))
            for g in range(HEADS):
                pe.wait_ge(S["pooled"], S.at("pooled", g))
                ins = pe.matmul(PS[:, 4 + g % 2, :], sm("pool_w")[:, g * P:(g + 1) * P], U[:, g, :, 16:16 + T],
                                start=True, stop=True)
                ins.then_inc(S["pool_out"], S.mark("pool_out", g))
                if g == 1:
                    pe.wait_ge(S["pool_scaled"], S.at("pool_scaled", 0))
                if g == 2:
                    pe.wait_ge(S["pool_scaled"], S.at("pool_scaled", 1))
            for h in range(HEADS):
                pe.wait_ge(S["o_squares"], S.at("o_squares", h))
                if h >= 2:
                    pe.wait_ge(S["o_rinv"], S.at("o_rinv", h - 2))
                if h < 2:
                    pe.wait_ge(S["pool_scaled"], S.at("pool_scaled", 3))
                pe.matmul(PS[:, 6 + h % 2, :], ONES, SQ[:, h, :], start=True, stop=True).then_inc(S["o_sums"], S.mark("o_sums", h))
            n0 = START["mix0_out"]
            pe.wait_ge(S["mixer_out0"], S.at("mixer_out0"))
            pe.wait_ge(S["pool_scaled"], S.at("pool_scaled", 3))
            for i in range(4):
                bank = 2 * (i % 4)
                pe_chunk_tokens_move(pe, n0 + i, CAT0, BOTH, bank, T2)

        def evac0(i):
            return ("taken_vector", i) if i in (8, 9, 10, 11) else ("taken_scalar", i)

        def act_mix0(act, order):
            n0 = START["mix0_in"]
            dests = {0: Q[:, 0:2, :], 1: Q[:, 2:4, :], 2: GS[:, 0:2, :], 3: GS[:, 2:4, :]}
            for i in range(4, 8):
                d, h = (i - 4) // 2, (i % 2) * 2
                dests[i] = K2[:, d, h * T2:(h + 2) * T2].rearrange("p (a b) -> p a b", a=2)
            for i in range(8):
                need_product(act, n0 + i)
                act.activation(dests[i], PS[:, 2 * (i % 3):2 * (i % 3) + 2, :], ACT.Silu if i < 4 else ACT.Sigmoid).then_inc(S["taken_scalar"], S.mark("taken_scalar", i))
            for d in range(2):
                act.wait_ge(S["forget"], S.at("forget", d))
                act.activation(B2[:, d, :], E2[:, d, :], ACT.Ln).then_inc(S["log_forget"], S.mark("log_forget", d))
            for i, (lv, d) in enumerate(STEPS):
                act.wait_ge(S["level_exponents"], S.at("level_exponents", i))
                act.activation(E2[:, i % 2, :], E2[:, i % 2, :], ACT.Exp).then_inc(S["level_decay"], S.mark("level_decay", i))
            act.wait_ge(S["level_products"], S.at("level_products", len(STEPS) - 1))
            for d in range(2):
                act.activation(W2[:, d, :], B2[:, d, :], ACT.Exp).then_inc(S["exp_b"], S.mark("exp_b", d))
            for d in range(2):
                last = B2[:, d, :].rearrange("p (n c) -> p n c", c=P)[:, :, 0 if d else P - 1]
                act.activation(TMP[:, d * 16:(d + 1) * 16], last, ACT.Exp).then_inc(S["exp_last"], S.mark("exp_last", d))
            for d in range(2):
                act.wait_ge(S["key_exponents"], S.at("key_exponents", d))
                act.activation(E2[:, d, :], E2[:, d, :], ACT.Exp).then_inc(S["key_decay"], S.mark("key_decay", d))
            for d in range(2):
                for j in range(3):
                    act.wait_ge(S["kt_ready"], S.at("kt_ready", (d, j)))
                    b = d * 3 + j if d * 3 + j < 4 else d * 3 + j - 4
                    act.activation(KT[:, d, j, :], PS[:, b, :], ACT.Identity).then_inc(S["kt"], S.mark("kt", (d, j)))
            for h in range(HEADS):
                act.wait_ge(S["mixed"], S.at("mixed", h))
                act.activation(SQ[:, h, :], PS[:, h, :], ACT.Square).then_inc(S["o_squares"], S.mark("o_squares", h))
            for g in range(HEADS):
                act.wait_ge(S["pool_out"], S.at("pool_out", g))
                act.activation(CAT0[:, g, :], PS[:, 4 + g % 2, :], ACT.Identity, scale=sm("pool_scale")[:, g:g + 1]).then_inc(S["pool_scaled"], S.mark("pool_scaled", g))
            for h in range(HEADS):
                act.wait_ge(S["o_sums"], S.at("o_sums", h))
                act.activation(SQ[:, 4 + h, :], PS[:, 6 + h % 2, :], ACT.Ln, scale=1.0 / P, bias=EPS[:, 0:1]).then_inc(order.sem, order.step())
                act.wait_ge(order.sem, order.n)
                act.activation(SQ[:, 4 + h, :], SQ[:, 4 + h, :], ACT.Exp, scale=-0.5).then_inc(S["o_rinv"], S.mark("o_rinv", h))

        def dve_mix0(dve, order):
            n0 = START["mix0_in"]
            for i in range(8, 12):
                need_product(dve, n0 + i)
                b = 2 * (i % 3)
                if i < 10:
                    src = PS[:, b:b + 2, :].rearrange("p b (t n) -> p (b t) n", t=2)
                    ins = dve.tensor_copy(V[:, :, (i - 8) * 256:(i - 7) * 256], src)
                else:
                    src = PS[:, b:b + 2, :].rearrange("p b (s n) -> p b s n", s=2)
                    if i == 10:
                        dve.wait_ge(S["pads"], S.at("pads"))
                    g = (i - 10) * 2
                    for j in range(2):
                        ins = dve.tensor_copy(U[:, g + j, :, 16:16 + T], src[:, j])
                        if j == 0:
                            ins.then_inc(order.sem, order.step())
                ins.then_inc(S["taken_vector"], S.mark("taken_vector", i))
            for d in range(2):
                for h in range(HEADS):
                    if h % 2 == 0:
                        dve.wait_ge(S["taken_scalar"], S.at("taken_scalar", 4 + 2 * d + h // 2))
                    lb, om = TMP[:, 32 + d * 4 + h:33 + d * 4 + h], TMP[:, 40 + d * 4 + h:41 + d * 4 + h]
                    ins = dve.tensor_scalar(E2[:, d, h * T2:(h + 1) * T2], K2[:, d, h * T2:(h + 1) * T2], om, lb, ALU.mult, ALU.add)
                    if h < 3:
                        ins.then_inc(order.sem, order.step())
                ins.then_inc(S["forget"], S.mark("forget", d))
            for d in range(2):
                dve.wait_ge(S["forget"], S.at("forget", d))
                dve.tensor_scalar(K2[:, d, :], E2[:, d, :], -1.0, 1.0, ALU.mult, ALU.add).then_inc(order.sem, order.step())
            dve.wait_ge(S["taken_vector"], S.at("taken_vector", 11))
            dve.memset(W2[:, 0, :], 1.0).then_inc(order.sem, order.step())
            dve.wait_ge(order.sem, order.n)
            dve.memset(W2[:, 0, :].rearrange("p (n c) -> p n c", c=P)[:, :, 0:1], 0.0).then_inc(order.sem, order.step())
            dve.wait_ge(order.sem, order.n)
            for d in range(2):
                dve.wait_ge(S["log_forget"], S.at("log_forget", d))
                b = B2[:, d, ::-1] if d else B2[:, d, :]
                dve.tensor_tensor_scan(b, W2[:, 0, :], b, 0.0, ALU.mult, ALU.add).then_inc(S["log_sums"], S.mark("log_sums", d))
            dve.tensor_tensor(E2[:, 0, :], K2[:, 0, :], K2[:, 1, :], ALU.add).then_inc(S["k_sum"], S.mark("k_sum"))
            dve.wait_ge(S["diag"], S.at("diag"))
            ident4 = bc(IDENT.unsqueeze(1), [P, NCH, P])
            for h in range(HEADS):
                dve.tensor_tensor(A[:, h, :].rearrange("p (c t) -> p c t", c=NCH),
                                             PS[:, h, :].rearrange("p (c t) -> p c t", c=NCH), ident4, ALU.mult).then_inc(order.sem, order.step())
            dve.wait_ge(order.sem, order.n)

            def take(i):
                lv, d = STEPS[i]
                dve.wait_ge(S["level_products"], S.at("level_products", i))
                if i:
                    dve.wait_ge(S["level_taken"], S.at("level_taken", i - 1))
                for h in range(HEADS):
                    m = M8[:, i * 256:(i + 1) * 256]
                    ins = dve.copy_predicated(halves(A[:, h, :], lv, 1 - d), m.rearrange("p (n h) -> p n h", h=1 << lv),
                                              PS[:, 4 + 2 * (i % 2) + h // 2, (h % 2) * 256:(h % 2 + 1) * 256]
                                              .rearrange("p (n h) -> p n h", h=1 << lv))
                    if h < HEADS - 1:
                        ins.then_inc(order.sem, order.step())
                ins.then_inc(S["level_taken"], S.mark("level_taken", i))

            qf = Q.rearrange("p a b -> p (a b)")
            for i, (lv, d) in enumerate(STEPS):
                dve.wait_ge(S["level_decay"], S.at("level_decay", i))
                if i >= 2:
                    dve.wait_ge(S["level_products"], S.at("level_products", i - 2))
                e, w = E2[:, i % 2, :], W2[:, i % 2, :]
                dve.tensor_tensor(halves(w, lv, d), halves(e, lv, d), halves(K2[:, d, :], lv, d), ALU.mult).then_inc(order.sem, order.step())
                dve.tensor_tensor(halves(w, lv, 1 - d), halves(e, lv, 1 - d), halves(qf, lv, 1 - d), ALU.mult).then_inc(S["level_operands"], S.mark("level_operands", i))
                if i >= 1:
                    take(i - 1)
            take(len(STEPS) - 1)
            for d in range(2):
                dve.wait_ge(S["key_decay"], S.at("key_decay", d))
                dve.tensor_tensor(E2[:, d, :], E2[:, d, :], K2[:, d, :], ALU.mult).then_inc(S["khat"], S.mark("khat", d))
            for d in range(2):
                dve.wait_ge(S["exp_b"], S.at("exp_b", d))
                ins = dve.tensor_tensor(W2[:, d, :], W2[:, d, :], qf, ALU.mult)
                if d == 0:
                    ins.then_inc(order.sem, order.step())
            ins.then_inc(S["qhat"], S.mark("qhat"))
            for d in range(2):
                dve.wait_ge(S["exp_last"], S.at("exp_last", d))
                for j in range(3):
                    dve.wait_ge(S["increment"], S.at("increment", (d, j)))
                    if j == 0:
                        ins = dve.tensor_copy(ST[:, d, 0, :], PS[:, 4, :])
                    else:
                        dve.wait_ge(S["state"], S.at("state", (d, j - 1)))
                        for h in range(HEADS):
                            hs = slice(h * P, (h + 1) * P)
                            e = TMP[:, d * 16 + h * 4 + ORD[d][j]:d * 16 + h * 4 + ORD[d][j] + 1]
                            ins = dve.scalar_tensor_tensor(out=ST[:, d, j, hs], in0=ST[:, d, j - 1, hs], scalar=e,
                                                           in1=PS[:, 4 + j, hs], op0=ALU.mult, op1=ALU.add)
                            if h < HEADS - 1:
                                ins.then_inc(order.sem, order.step())
                    ins.then_inc(S["state"], S.mark("state", (d, j)))
            for h in range(HEADS):
                dve.wait_ge(S["o_rinv"], S.at("o_rinv", h))
                dve.scalar_tensor_tensor(out=SQ[:, 4 + h, :], in0=PS[:, h, :], scalar=sm("onorm"), in1=SQ[:, 4 + h, :],
                                                   op0=ALU.mult, op1=ALU.mult).then_inc(order.sem, order.step())
                dve.wait_ge(order.sem, order.n)
                ins = dve.tensor_tensor(GS[:, h, :], GS[:, h, :], SQ[:, 4 + h, :], ALU.mult)
                if h < HEADS - 1:
                    ins.then_inc(order.sem, order.step())
            ins.then_inc(S["mixer_out0"], S.mark("mixer_out0"))
            for i in range(4):
                need_product(dve, START["mix0_out"] + i)
                dve.tensor_copy(K2.rearrange("p d (a b) -> p (d a) b", a=HEADS)[:, 2 * i:2 * i + 2, :],
                                       PS[:, 2 * i:2 * i + 2, :]).then_inc(S["taken_out0"], S.mark("taken_out0", i))

        Y0 = arena(4096, DT, T2)

        def pool_mix0(pool, order):
            pool.memset(U[:, :, :, 0:16], 0.0).then_inc(order.sem, order.step())
            pool.memset(U[:, :, :, 16 + T:], 0.0).then_inc(S["pads"], S.mark("pads"))
            pool.wait_ge(S["counts_loaded"], S.at("counts_loaded"))
            pool.wait_ge(S["taken_vector"], S.at("taken_vector", 11))
            for g in range(HEADS):
                u = U[:, g, :, :]
                at = lambda ap, lo, n: ap[:, :, 16 + lo:16 + lo + n]
                lo, n, src, dst = -15, T + 31, u, SA
                if g:
                    pool.wait_ge(S["pooled"], S.at("pooled", g - 1))
                pool.tensor_tensor(at(SA, -15, T + 31), at(u, -16, T + 31), at(u, -15, T + 31), ALU.add).then_inc(order.sem, order.step())
                pool.wait_ge(order.sem, order.n)
                src, other = SA, SB
                for m in range(1, g + 1):
                    w = 1 << (m - 1)
                    lo, n = lo + w, n - 2 * w
                    pool.tensor_tensor(at(other, lo, n), at(src, lo - w, n), at(src, lo + w, n), ALU.add).then_inc(order.sem, order.step())
                    pool.wait_ge(order.sem, order.n)
                    src, other = other, src
                pool.tensor_tensor(at(src, 0, T), at(src, 0, T), bc(INVC[:, g, :].unsqueeze(1), [P, 2, T]), ALU.mult).then_inc(order.sem, order.step())
                pool.wait_ge(order.sem, order.n)
                pool.tensor_tensor(at(u, 0, T), at(src, 0, T), at(u, 0, T), ALU.subtract).then_inc(S["pooled"], S.mark("pooled", g))

            pool.wait_ge(S["log_sums"], S.at("log_sums", 1))
            for i, (lv, d) in enumerate(STEPS):
                if i == 0:
                    pool.wait_ge(S["diag"], S.at("diag"))
                if i == 1:
                    pool.wait_ge(S["diag"], S.at("diag"))
                if i >= 2:
                    pool.wait_ge(S["level_operands"], S.at("level_operands", i - 2))
                b, e, hb = B2[:, d, :], E2[:, i % 2, :], 1 << lv
                n = HEADS * T2 // (2 * hb)
                ref = bc(halves(b, lv, d)[:, :, (0 if d else hb - 1):(1 if d else hb)], [P, n, hb])
                pool.tensor_tensor(halves(e, lv, d), ref, halves(b, lv, d), ALU.subtract).then_inc(order.sem, order.step())
                pool.tensor_tensor(halves(e, lv, 1 - d), halves(b, lv, 1 - d), ref, ALU.subtract).then_inc(S["level_exponents"], S.mark("level_exponents", i))
            for d in range(2):
                pool.wait_ge(S["level_operands"], S.at("level_operands", len(STEPS) - 2 + d))
                b = B2[:, d, :].rearrange("p (n c) -> p n c", c=P)
                last = bc(b[:, :, (0 if d else P - 1):(1 if d else P)], [P, HEADS * NCH, P])
                pool.tensor_tensor(E2[:, d, :].rearrange("p (n c) -> p n c", c=P), last, b, ALU.subtract).then_inc(S["key_exponents"], S.mark("key_exponents", d))
        AH, AKV = 8, 2
        QR = arena(0, AH, T)
        KR = arena(2048, AKV, T2)
        VV = arena(3072, NCH, AKV * P)
        RN = arena(4096, 6, T2)
        COS, SIN = arena(7168, T), arena(7424, T)
        RT = arena(7680, 2, T)
        PR = arena(8192, 2, T2)
        PT = arena(9216, 2, NCH, T)
        CAT1 = arena(11264, AH, T)
        NEGMAX, PSUM_OF, RECIP = (arena(13312 + 16 * i, 16) for i in range(3))
        UNITS = 2 * AH
        ROPE_BANKS = [6, 7, 0, 1, 2]
        QUERY_SCALE = float(P) ** -0.5

        def pe_mix1(pe):
            n0 = START["mix1_in"]
            pe.wait_ge(S["normed"], S.at("normed", "mix1"))
            pe.wait_ge(S["rinv"], S.at("rinv", "mix1"))
            pe_chunk_tokens_move(pe, n0, H, BOTH, 0, T2)
            pe_chunk_tokens_stay(pe, n0 + 1, H, 0, NCH, 2)
            for i in range(2, 6):
                pe_chunk_tokens_move(pe, n0 + i, H, LAT, i + 2, T)
            pe.wait_ge(S["values_taken"], S.at("values_taken"))
            for u in range(6):
                pe.wait_ge(S["head_squares"], S.at("head_squares", 0 if u < 2 else u - 1))
                if u >= 4:
                    pe.wait_ge(S["head_squares"], S.at("head_squares", u - 3))
                pe.matmul(PS[:, u, :], ONES, SQ[:, u, :], start=True, stop=True).then_inc(S["head_sums"], S.mark("head_sums", u))
            for u in range(5):
                pe.wait_ge(S["head_normed"], S.at("head_normed", u))
                if u >= 1:
                    pe.wait_ge(S["head_rinv"], S.at("head_rinv", 5))
                rhs = KR[:, :, LAT] if u == 0 else QR[:, 2 * u - 2:2 * u, :]
                pe.matmul(PS[:, ROPE_BANKS[u], :], ROPE, rhs, start=True, stop=True).then_inc(S["rope_swapped"], S.mark("rope_swapped", u))

            def scores(i):
                h, tt = i // 2, i % 2
                pe.wait_ge(S["rotated"], S.at("rotated", 0))
                pe.wait_ge(S["rotated"], S.at("rotated", 1 + h // 2))
                if i >= 2:
                    pe.wait_ge(S["probs"], S.at("probs", i - 2))
                pe.matmul(PS[:, 3 + i % 2, :], QR[:, h, tt * P:(tt + 1) * P], KR[:, h // 4, :], start=True, stop=True).then_inc(S["scores"], S.mark("scores", i))

            def values(i):
                h, tt = i // 2, i % 2
                pe.wait_ge(S["probs_scaled"], S.at("probs_scaled", i))
                if i >= 2:
                    pe.wait_ge(S["probs_turned"], S.at("probs_turned", i - 2))
                for st in range(NCH):
                    ins = pe.transpose(PS[:, 5 + i % 2, st * P:(st + 1) * P], PR[:, i % 2, st * P:(st + 1) * P], IDENT)
                ins.then_inc(S["turned"], S.mark("turned", i))

            def mix(h):
                pe.wait_ge(S["probs_turned"], S.at("probs_turned", 2 * h + 1))
                hp = h // 2
                if h % 2 == 0 and hp >= 2:
                    pe.wait_ge(S["heads_taken"], S.at("heads_taken", hp - 2))
                for st in range(NCH):
                    ins = pe.matmul(PS[:, (7, 0)[hp % 2], (h % 2) * T:(h % 2 + 1) * T], VV[:, st, (h // 4) * P:(h // 4 + 1) * P],
                                    PT[:, h % 2, st, :], start=(st == 0), stop=(st == NCH - 1))
                ins.then_inc(S["head_mixed"], S.mark("head_mixed", h))

            pe.wait_ge(S["rotated"], S.at("rotated", 4))
            scores(0)
            for i in range(UNITS):
                if i + 1 < UNITS:
                    scores(i + 1)
                values(i)
                if i % 2 == 0 and i >= 2:
                    mix(i // 2 - 1)
            mix(AH - 1)
            pe.wait_ge(S["heads_taken"], S.at("heads_taken", 3))
            for i in range(4):
                pe_chunk_tokens_move(pe, START["mix1_out"] + i, CAT1, slice(0, T), i, T)

        def act_mix1(act, order):
            n0 = START["mix1_in"]
            need_product(act, n0)
            act.activation(KR[:, :, :], PS[:, 0:2, :], ACT.Identity).then_inc(order.sem, order.step())
            act.activation(SQ[:, 0:2, :], PS[:, 0:2, :], ACT.Square).then_inc(S["head_squares"], S.mark("head_squares", 0))
            for i in range(2, 6):
                need_product(act, n0 + i)
                act.activation(QR[:, 2 * i - 4:2 * i - 2, :].rearrange("p a b -> p (a b)"), PS[:, i + 2, :], ACT.Identity).then_inc(order.sem, order.step())
                act.activation(SQ[:, i, :], PS[:, i + 2, :], ACT.Square).then_inc(S["head_squares"], S.mark("head_squares", i - 1))
            for u in range(6):
                act.wait_ge(S["head_sums"], S.at("head_sums", u))
                act.activation(RN[:, u, :], PS[:, u, :], ACT.Ln, scale=1.0 / P, bias=EPS[:, 0:1]).then_inc(order.sem, order.step())
            act.wait_ge(order.sem, order.n)
            for u in range(6):
                act.activation(RN[:, u, :], RN[:, u, :], ACT.Exp, scale=-0.5).then_inc(S["head_rinv"], S.mark("head_rinv", u))

            def exps(i):
                act.wait_ge(S["neg_max"], S.at("neg_max", i))
                if i >= 2:
                    act.wait_ge(S["turned"], S.at("turned", i - 2))
                act.activation(PR[:, i % 2, :], PS[:, 3 + i % 2, :], ACT.Exp, bias=NEGMAX[:, i:i + 1],
                                      scale=QUERY_SCALE, accum_out=PSUM_OF[:, i:i + 1]).then_inc(S["probs"], S.mark("probs", i))

            exps(0)
            for i in range(UNITS):
                if i + 1 < UNITS:
                    exps(i + 1)
                act.wait_ge(S["turned"], S.at("turned", i))
                h, tt = i // 2, i % 2
                if h >= 2:
                    act.wait_ge(S["head_mixed"], S.at("head_mixed", h - 2))
                act.activation(PT[:, h % 2, :, tt * P:(tt + 1) * P], PS[:, 5 + i % 2, :].rearrange("p (s t) -> p s t", t=P),
                                      ACT.Identity).then_inc(S["probs_turned"], S.mark("probs_turned", i))

        def dve_mix1(dve, order):
            n0 = START["mix1_in"]
            need_product(dve, n0 + 1)
            dve.tensor_copy(VV[:, :, :], PS[:, 2:4, :].rearrange("p b (t n) -> p (b t) n", t=2)).then_inc(S["values_taken"], S.mark("values_taken"))
            for u in range(5):
                dve.wait_ge(S["head_rinv"], S.at("head_rinv", 1 if u == 0 else u + 1))
                x = KR[:, :, :] if u == 0 else QR[:, 2 * u - 2:2 * u, :]
                r = RN[:, 0:2, :] if u == 0 else RN[:, u + 1, :].rearrange("p (a b) -> p a b", a=2)
                dve.scalar_tensor_tensor(out=x, in0=x, scalar=sm("knorm" if u == 0 else "qnorm"), in1=r,
                                                op0=ALU.mult, op1=ALU.mult).then_inc(S["head_normed"], S.mark("head_normed", u))
            dve.wait_ge(S["rope_loaded"], S.at("rope_loaded"))
            cos, sin = (bc(a.unsqueeze(1), [P, 2, T]) for a in (COS, SIN))
            for u in range(5):
                dve.wait_ge(S["rope_swapped"], S.at("rope_swapped", u))
                x = KR[:, :, LAT] if u == 0 else QR[:, 2 * u - 2:2 * u, :]
                if u:
                    dve.wait_ge(S["rotated"], S.at("rotated", u - 1))
                dve.tensor_tensor(RT, PS[:, ROPE_BANKS[u], :].rearrange("p (a b) -> p a b", a=2), sin, ALU.mult).then_inc(order.sem, order.step())
                dve.tensor_tensor(x, x, cos, ALU.mult).then_inc(order.sem, order.step())
                dve.wait_ge(order.sem, order.n)
                dve.tensor_tensor(x, x, RT, ALU.add).then_inc(S["rotated"], S.mark("rotated", u))

            def maxima(i):
                dve.wait_ge(S["scores"], S.at("scores", i))
                dve.tensor_reduce(NEGMAX[:, i:i + 1], PS[:, 3 + i % 2, :], AX.X, ALU.max).then_inc(order.sem, order.step())
                dve.wait_ge(order.sem, order.n)
                dve.tensor_scalar(NEGMAX[:, i:i + 1], NEGMAX[:, i:i + 1], -QUERY_SCALE, None, ALU.mult).then_inc(S["neg_max"], S.mark("neg_max", i))

            maxima(0)
            for i in range(UNITS):
                if i + 1 < UNITS:
                    maxima(i + 1)
                dve.wait_ge(S["probs"], S.at("probs", i))
                dve.reciprocal(RECIP[:, i:i + 1], PSUM_OF[:, i:i + 1]).then_inc(order.sem, order.step())
                dve.wait_ge(order.sem, order.n)
                dve.tensor_scalar(PR[:, i % 2, :], PR[:, i % 2, :], RECIP[:, i:i + 1], None, ALU.mult).then_inc(S["probs_scaled"], S.mark("probs_scaled", i))
                if i % 4 == 2 and i > 2:
                    take_heads(dve, i // 4 - 1)
            take_heads(dve, 3)

        def take_heads(dve, hp):
            dve.wait_ge(S["head_mixed"], S.at("head_mixed", 2 * hp + 1))
            dve.tensor_copy(CAT1[:, 2 * hp:2 * hp + 2, :].rearrange("p a b -> p (a b)"), PS[:, (7, 0)[hp % 2], :]).then_inc(S["heads_taken"], S.mark("heads_taken", hp))

        ACC = PS[:, 0:4, :].rearrange("p b (m t) -> p (b m) t", t=T)
        XL = X[:, :, LAT]

        def pe_layernorm(pe, tag):
            pe.wait_ge(S["summed"], S.at("summed", tag))
            pe_sum_features(pe, (tag, "mean"), [X[:, k, LAT] for k in range(DT)], T)
            pe.wait_ge(S["centred"], S.at("centred", tag))
            pe_norm(pe, tag, LAT)

        def act_layernorm(act, order, tag):
            act.wait_ge(S["centred"], S.at("centred", tag))
            act_squares(act, tag, XL, LAT)
            act_rinv(act, order, tag, T, D, 1)

        def dve_layernorm(dve, order, tag, coef, g):
            dve.scalar_tensor_tensor(out=XL, in0=ACC, scalar=coef / ALPHA, in1=XL, op0=ALU.mult, op1=ALU.add).then_inc(S["summed"], S.mark("summed", tag))
            dve.wait_ge(S["feature_sums"], S.at("feature_sums", (tag, "mean")))
            mean = bc(PS[:, 7, 0:T].unsqueeze(1), [P, DT, T])
            dve.wait_ge(S["summed"], S.at("summed", tag))
            dve.scalar_tensor_tensor(out=XL, in0=mean, scalar=-1.0 / D, in1=XL, op0=ALU.mult, op1=ALU.add).then_inc(S["centred"], S.mark("centred", tag))
            dve.wait_ge(S["rinv"], S.at("rinv", tag))
            dve.tensor_tensor(SQ[:, :, LAT], XL, rows(0, T), ALU.mult).then_inc(order.sem, order.step())
            dve.wait_ge(order.sem, order.n)
            for k in range(DT):
                ins = dve.tensor_scalar(X[:, k, LAT], SQ[:, k, LAT], sm("ln_g")[:, g * 8 + k:g * 8 + k + 1],
                                        sm("ln_b")[:, g * 8 + k:g * 8 + k + 1], ALU.mult, ALU.add)
                if k < DT - 1:
                    ins.then_inc(order.sem, order.step())
            ins.then_inc(S["ln_out"], S.mark("ln_out", tag))
            dve.wait_ge(S["ln_out"], S.at("ln_out", tag))

        PEMB = arena(20736, 2, 2, T)

        def pe_ple(pe, l):
            n0 = START[f"ple{l}"]
            for i in range(4):
                pe_chunk_tokens_move(pe, n0 + i, X, LAT, i, T)
            need_chunk(pe, n0 + 4)
            pe.wait_ge(S["emb_loaded"], S.at("emb_loaded", l))
            for m in range(DT):
                for k in range(2):
                    ins = pe.matmul(PS[:, 4 + m // 2, (m % 2) * T:(m % 2 + 1) * T],
                                    ring[:, (n0 + 4) % SLOTS, k * D + m * P:k * D + (m + 1) * P], PEMB[:, l - 2, k, :],
                                    start=(k == 0), stop=(k == 1))
            ins.then_inc(multiplied, 1)

        def act_ple(act, order, l):
            for m in range(DT):
                need_product(act, START[f"ple{l}"] + m // 2)
                b = (l - 2) * 8 + m
                act.activation(SQ[:, m, LAT], ACC[:, m, :], ACT.Sigmoid, bias=sm("ple_bg")[:, b:b + 1]).then_inc(S["ple_gate"], S.mark("ple_gate", (l, m)))

        def dve_ple(dve, order, l):
            need_product(dve, START[f"ple{l}"] + 4)
            dve.wait_ge(S["ple_gate"], S.at("ple_gate", (l, DT - 1)))
            dve.tensor_tensor(SQ[:, :, LAT], SQ[:, :, LAT], PS[:, 4:8, :].rearrange("p b (m t) -> p (b m) t", t=T), ALU.mult).then_inc(order.sem, order.step())
            dve.wait_ge(order.sem, order.n)
            dve.tensor_tensor(XL, XL, SQ[:, :, LAT], ALU.add).then_inc(S["ple_out"], S.mark("ple_out", l))
            dve.wait_ge(S["ple_out"], S.at("ple_out", l))

        WH, KEYS = 8, 384
        KV = arena(0, 512)
        QW = arena(512, 4, T)
        BXR = arena(1536, 4, T)
        BX = arena(2560, 4, T)
        BG = arena(3584, 4, T)
        BIAS = arena(4608, WH, KEYS)
        SC = arena(7680, WH, KEYS)
        PTW = arena(10752, WH, KEYS)
        CAT2 = arena(13824, DT, T)
        GR, GI = arena(15872, 4, T), arena(16896, 4, T)
        LA, TH = arena(17920, 4, T), arena(18944, 4, T)
        WAX = H[:, 0:2, :].rearrange("p a (i n) -> p (a i) n", i=4)
        MW, NMW, ESW, SUMW, DENW = (arena(19968 + 16 * i, WH, 2) for i in range(5))
        SPL = arena(20048, 4, 4)
        flat = lambda ap: ap.rearrange("p a b -> p (a b)")

        def blocks(ap):
            return ap[:, :, 0:P], ap[:, :, P:KEYS]

        SCORE_BANKS = [7, 0, 1, 2]

        def pe_mix2(pe):
            n0 = START["mix2_in"]
            need_chunk(pe, n0)
            w = lambda k, j: ring[:, n0 % SLOTS, k * 256 + j * P:k * 256 + (j + 1) * P]
            for k in range(DT):
                pe.matmul(PS[:, 0, 0:T], w(k, 0), X[:, k, LAT], start=(k == 0), stop=(k == DT - 1))
            for t in range(2):
                for k in range(DT):
                    ins = pe.matmul(PS[:, 0, T + t * P:T + (t + 1) * P], X[:, k, T + t * P:T + (t + 1) * P], w(k, 1),
                                    start=(k == 0), stop=(k == DT - 1))
            ins.then_inc(multiplied, 1)
            for i in range(1, 7):
                pe_chunk_tokens_move(pe, n0 + i, X, LAT, i, T)
            pe.wait_ge(S["kv_taken"], S.at("kv_taken"))
            for h in range(WH):
                j, g = h % 4, 64 * (h // 4)
                if h < 4:
                    pe.wait_ge(S["queries_taken"], S.at("queries_taken", 1))
                else:
                    pe.wait_ge(S["biased"], S.at("biased", h - 4))
                b = SCORE_BANKS[h % 4]
                pe.matmul(PS[:, b, 0:P], QW[g:g + 64, j, 0:P], KV[g:g + 64, 0:P], start=True, stop=True)
                pe.matmul(PS[:, b, P:KEYS], QW[g:g + 64, j, P:T], KV[g:g + 64, 0:T], start=True, stop=True).then_inc(S["wscores"], S.mark("wscores", h))
            pe.wait_ge(S["gelu"], S.at("gelu", 1))
            pe.wait_ge(S["conv"], S.at("conv"))
            pe.wait_ge(S["gates_loaded"], S.at("gates_loaded"))
            for g in range(2):
                for i in range(4):
                    ins = pe.matmul(PS[:, 3 + 2 * g + i // 2, (i % 2) * T:(i % 2 + 1) * T], WAX[:, 4 * g + i, :], BX[:, i, :],
                                    start=True, stop=True)
            ins.then_inc(S["gate_products"], S.mark("gate_products"))
            for h in range(WH):
                pe.wait_ge(S["wprobs_scaled"], S.at("wprobs_scaled"))
                if h >= 4:
                    pe.wait_ge(S["wturned"], S.at("wturned", h - 4))
                for c in range(3):
                    ins = pe.transpose(PS[:, SCORE_BANKS[h % 4], c * P:(c + 1) * P], SC[:, h, c * P:(c + 1) * P], IDENT)
                ins.then_inc(S["wturn"], S.mark("wturn", h))
            pe.wait_ge(S["gates_sigmoid"], S.at("gates_sigmoid"))
            for h in range(WH):
                j, g = h % 4, 64 * (h // 4)
                pe.wait_ge(S["wturned"], S.at("wturned", h))
                v = lambda t: KV[:, T + t * P + g:T + t * P + g + 64]
                o = PS[g:g + 64, 3 + j // 2, :]
                c = (j % 2) * T
                pe.matmul(o[:, c:c + P], v(0), PTW[:, h, 0:P], start=True, stop=True)
                pe.matmul(o[:, c + P:c + T], v(0), PTW[:, h, P:2 * P], start=True, stop=False)
                ins = pe.matmul(o[:, c + P:c + T], v(1), PTW[:, h, 2 * P:KEYS], start=False, stop=True)
            ins.then_inc(S["wmixed"], S.mark("wmixed"))
            pe.wait_ge(S["cat2"], S.at("cat2"))
            for i in range(4):
                pe_chunk_tokens_move(pe, START["mix2_out"] + i, CAT2, slice(0, T), i, T)

        def act_mix2(act, order):
            n0 = START["mix2_in"]
            need_product(act, n0)
            act.activation(KV, PS[:, 0, :], ACT.Identity).then_inc(S["kv_taken"], S.mark("kv_taken"))
            for i in range(2):
                need_product(act, n0 + 1 + i)
                act.activation(flat(QW[:, 2 * i:2 * i + 2, :]), PS[:, 1 + i, :], ACT.Identity).then_inc(S["queries_taken"], S.mark("queries_taken", i))
            for i in range(2):
                need_product(act, n0 + 5 + i)
                act.activation(flat(BG[:, 2 * i:2 * i + 2, :]), PS[:, 5 + i, :], ACT.Gelu_apprx_tanh).then_inc(S["gelu"], S.mark("gelu", i))
            act.wait_ge(S["neg_abs_lam"], S.at("neg_abs_lam"))
            act.activation(SPL[:, 1, :], SPL[:, 1, :], ACT.Exp).then_inc(order.sem, order.step())
            act.wait_ge(order.sem, order.n)
            act.activation(SPL[:, 1, :], SPL[:, 1, :], ACT.Ln, bias=EPS[:, 2:3]).then_inc(S["softplus_tail"], S.mark("softplus_tail"))
            act.wait_ge(S["sink_less_max"], S.at("sink_less_max"))
            act.activation(ESW, ESW, ACT.Exp).then_inc(S["exp_sink"], S.mark("exp_sink"))
            for h in range(WH):
                for tt in range(2):
                    s = blocks(SC)[tt][:, h, :]
                    ins = act.activation(s, s, ACT.Exp, bias=NMW[:, h, tt:tt + 1], accum_out=SUMW[:, h, tt:tt + 1])
                    if (h, tt) != (WH - 1, 1):
                        ins.then_inc(order.sem, order.step())
            ins.then_inc(S["wprobs"], S.mark("wprobs"))
            act.wait_ge(S["gate_products"], S.at("gate_products"))
            for g, (dst, bias) in enumerate(((GR, "b_ba"), (GI, "b_bx"))):
                for i in range(4):
                    ins = act.activation(dst[:, i, :], PS[:, 3 + 2 * g + i // 2, (i % 2) * T:(i % 2 + 1) * T], ACT.Sigmoid,
                                         bias=sm(bias)[:, i:i + 1])
                    if (g, i) != (1, 3):
                        ins.then_inc(order.sem, order.step())
            ins.then_inc(S["gates_sigmoid"], S.mark("gates_sigmoid"))
            act.wait_ge(S["log_a"], S.at("log_a"))
            act.activation(TH, LA, ACT.Tanh, scale=-1.0).then_inc(S["tanh_a"], S.mark("tanh_a"))
            act.wait_ge(S["tanh_a"], S.at("tanh_a"))
            act.activation(LA, LA, ACT.Exp).then_inc(S["decay_a"], S.mark("decay_a"))
            for h in range(WH):
                act.wait_ge(S["wturn"], S.at("wturn", h))
                act.activation(PTW[:, h, :], PS[:, SCORE_BANKS[h % 4], 0:KEYS], ACT.Identity).then_inc(S["wturned"], S.mark("wturned", h))
            act.wait_ge(S["one_less_a2"], S.at("one_less_a2"))
            act.activation(TH, TH, ACT.Sqrt).then_inc(S["root"], S.mark("root"))

        def dve_mix2(dve, order):
            n0 = START["mix2_in"]
            dve.tensor_scalar(SPL[:, 0, :], sm("b_lam"), -1.0, 0.0, ALU.mult, ALU.max).then_inc(order.sem, order.step())
            dve.wait_ge(order.sem, order.n)
            dve.tensor_scalar(SPL[:, 2, :], sm("b_lam"), 0.0, None, ALU.min).then_inc(order.sem, order.step())
            dve.wait_ge(order.sem, order.n)
            dve.tensor_scalar(SPL[:, 3, :], sm("b_lam"), 0.0, None, ALU.max).then_inc(order.sem, order.step())
            dve.wait_ge(order.sem, order.n)
            dve.tensor_tensor(SPL[:, 1, :], SPL[:, 2, :], SPL[:, 3, :], ALU.subtract).then_inc(S["neg_abs_lam"], S.mark("neg_abs_lam"))
            for i in range(4):
                if i % 2 == 0:
                    need_product(dve, n0 + 3 + i // 2)
                x = PS[:, 3 + i // 2, (i % 2) * T:(i % 2 + 1) * T]
                tap = lambda j: sm("b_conv")[:, j * 4 + i:j * 4 + i + 1]
                dve.tensor_scalar(BX[:, i, :], x, tap(3), sm("conv_b")[:, i:i + 1], ALU.mult, ALU.add).then_inc(order.sem, order.step())
                dve.wait_ge(order.sem, order.n)
                for j in (2, 1, 0):
                    lag = 3 - j
                    ins = dve.scalar_tensor_tensor(out=BX[:, i, lag:], in0=x[:, 0:T - lag], scalar=tap(j), in1=BX[:, i, lag:],
                                                   op0=ALU.mult, op1=ALU.add)
                    if (i, j) == (3, 0):
                        ins.then_inc(S["conv"], S.mark("conv"))
                    else:
                        ins.then_inc(order.sem, order.step())
                        dve.wait_ge(order.sem, order.n)
            dve.wait_ge(S["bias_loaded"], S.at("bias_loaded"))
            for h in range(WH):
                dve.wait_ge(S["wscores"], S.at("wscores", h))
                dve.scalar_tensor_tensor(out=SC[:, h, :], in0=PS[:, SCORE_BANKS[h % 4], 0:KEYS], scalar=0.125,
                                                in1=BIAS[:, h, :], op0=ALU.mult, op1=ALU.add).then_inc(S["biased"], S.mark("biased", h))
            dve.wait_ge(S["biased"], S.at("biased", WH - 1))
            for tt in range(2):
                dve.tensor_reduce(MW[:, :, tt], blocks(SC)[tt], AX.X, ALU.max).then_inc(order.sem, order.step())
            dve.wait_ge(order.sem, order.n)
            sink = bc(sm("sinks").unsqueeze(2), [P, WH, 2])
            dve.tensor_tensor(MW, MW, sink, ALU.max).then_inc(order.sem, order.step())
            dve.wait_ge(order.sem, order.n)
            dve.tensor_scalar(NMW, MW, -1.0, None, ALU.mult).then_inc(order.sem, order.step())
            dve.tensor_tensor(ESW, sink, MW, ALU.subtract).then_inc(S["sink_less_max"], S.mark("sink_less_max"))
            dve.wait_ge(S["wprobs"], S.at("wprobs"))
            dve.tensor_tensor(DENW, SUMW, ESW, ALU.add).then_inc(order.sem, order.step())
            dve.wait_ge(order.sem, order.n)
            dve.reciprocal(DENW, DENW).then_inc(order.sem, order.step())
            dve.wait_ge(order.sem, order.n)
            for tt in range(2):
                s = blocks(SC)[tt]
                ins = dve.tensor_tensor(s, s, bc(DENW[:, :, tt:tt + 1], [P, WH, s.shape[2]]), ALU.mult)
                if tt == 0:
                    ins.then_inc(order.sem, order.step())
            ins.then_inc(S["wprobs_scaled"], S.mark("wprobs_scaled"))
            dve.wait_ge(S["softplus_tail"], S.at("softplus_tail"))
            dve.tensor_tensor(SPL[:, 2, :], SPL[:, 0, :], SPL[:, 1, :], ALU.add).then_inc(order.sem, order.step())
            dve.wait_ge(order.sem, order.n)
            dve.tensor_scalar(SPL[:, 2, :], SPL[:, 2, :], -8.0, None, ALU.mult).then_inc(order.sem, order.step())
            dve.wait_ge(order.sem, order.n)
            dve.wait_ge(S["gates_sigmoid"], S.at("gates_sigmoid"))
            for i in range(4):
                ins = dve.tensor_scalar(LA[:, i, :], GR[:, i, :], SPL[:, 2, i:i + 1], None, ALU.mult)
                if i < 3:
                    ins.then_inc(order.sem, order.step())
            ins.then_inc(S["log_a"], S.mark("log_a"))
            dve.tensor_tensor(GI, GI, BX, ALU.mult).then_inc(order.sem, order.step())
            dve.wait_ge(order.sem, order.n)
            dve.wait_ge(S["decay_a"], S.at("decay_a"))
            dve.tensor_tensor(GR, LA, LA, ALU.mult).then_inc(order.sem, order.step())
            dve.wait_ge(order.sem, order.n)
            dve.scalar_tensor_tensor(out=TH, in0=GR, scalar=1.0, in1=TH, op0=ALU.add, op1=ALU.mult).then_inc(S["one_less_a2"], S.mark("one_less_a2"))
            dve.wait_ge(S["root"], S.at("root"))
            dve.tensor_tensor(GI, GI, TH, ALU.mult).then_inc(order.sem, order.step())
            dve.wait_ge(order.sem, order.n)
            dve.memset(LA[:, :, 0:1], 0.0).then_inc(order.sem, order.step())
            dve.wait_ge(order.sem, order.n)
            dve.tensor_tensor_scan(flat(GR), flat(LA), flat(GI), 0.0, ALU.mult, ALU.add).then_inc(order.sem, order.step())
            dve.wait_ge(order.sem, order.n)
            dve.tensor_tensor(CAT2[:, 4:8, :], GR, BG, ALU.mult).then_inc(order.sem, order.step())
            dve.wait_ge(S["wmixed"], S.at("wmixed"))
            dve.tensor_copy(flat(CAT2[:, 0:4, :]), PS[:, 3:5, :].rearrange("p a b -> p (a b)")).then_inc(S["cat2"], S.mark("cat2"))
        DH, LV3 = 8, LEVELS
        QKV = arena(0, 24, T)
        QD, KD3, VD = QKV[:, 0:8, :], QKV[:, 8:16, :], QKV[:, 16:24, :]
        ZS = arena(6144, DH, T)
        RN3 = arena(8192, 8, T2)
        XI, XT = arena(8192, 4, T2), arena(10240, 4, T2)
        QG, KBG = arena(12288, DH, T), arena(14336, DH, T)
        DM = arena(16384, DH, T)
        LT = arena(18432, DH, T)
        AT = arena(20480, DH, T)
        ROWS = arena(22528, 2, T)
        GROW, BROW = ROWS[0:DH, 0, :], ROWS[0:DH, 1, :]
        W8 = arena(23040, 4, T)
        COLS = arena(24064, 2, 3, DH)
        NA = TMP[0:DH, 0:2]
        ZT, CT = SQ[:, 0:4, :], SQ[:, 4:8, :]
        VB, KDEC = (H[:, 4 * i:4 * i + 4, :].rearrange("p a (b n) -> p (a b) n", b=4) for i in range(2))
        OD = arena(0, DH, T)
        ST3 = arena(16384, DH * P)
        RV = arena(18432, 2, DH * P)
        NEGL = X[:, 0:4, CTX]

        def unit(i):
            return i // 4, slice((i % 4) * P, (i % 4 + 1) * P)

        def pe_mix3(pe):
            n0 = START["mix3_in"]
            for j in range(2):
                for k in range(DT):
                    ins = pe.matmul(PS[0:DH, 7, j * T:(j + 1) * T], sm("w_ba")[:, k * 16 + j * 8:k * 16 + (j + 1) * 8], X[:, k, LAT],
                                    start=(k == 0), stop=(k == DT - 1))
            ins.then_inc(S["logits"], S.mark("logits"))
            for i in range(16):
                if i >= 6:
                    pe.wait_ge(S["conv3" if i - 6 < 12 else "z_taken"], S.at("conv3" if i - 6 < 12 else "z_taken", i - 6))
                pe_chunk_tokens_move(pe, n0 + i, X, LAT, i % 6, T)
            pe.wait_ge(S["rows3"], S.at("rows3"))
            for c in range(2):
                for j, src in enumerate((GROW, BROW, W8[0:DH, 0, :])):
                    ins = pe.transpose(PS[:, 7, (3 * c + j) * DH:(3 * c + j + 1) * DH], src[:, c * P:(c + 1) * P], IDENT[0:DH, 0:DH])
            ins.then_inc(S["cols3"], S.mark("cols3"))
            pe.wait_ge(S["z_taken"], S.at("z_taken", 15))
            pe.wait_ge(S["conv3"], S.at("conv3", 11))
            for u in range(8):
                pe.wait_ge(S["qk_squares"], S.at("qk_squares", u))
                if u >= 6:
                    pe.wait_ge(S["cols_taken"], S.at("cols_taken"))
                    pe.wait_ge(S["qk_rinv"], S.at("qk_rinv", u - 6))
                pe.matmul(PS[:, (0, 1, 2, 3, 4, 5, 0, 1)[u], :], ONES, SQ[:, u, :], start=True, stop=True).then_inc(S["qk_sums"], S.mark("qk_sums", u))
            pe.wait_ge(S["qk_rinv"], S.at("qk_rinv", 7))
            for i in range(8):
                which, g = i // 4, i % 4
                src = (VD, KD3)[which]
                if which:
                    pe.wait_ge(S["k_normed"], S.at("k_normed", 3))
                    pe.wait_ge(S["side_taken"], S.at("side_taken", i - 4))
                else:
                    pe.wait_ge(S["conv_silu"], S.at("conv_silu", 8 + g))
                for u in range(4 * g, 4 * g + 4):
                    ins = pe.transpose(PS[:, 2 + g, unit(u)[1]], src[:, u // 2, (u % 2) * P:(u % 2 + 1) * P], IDENT)
                ins.then_inc(S["side_turned"], S.mark("side_turned", i))
            for h in range(DH):
                pe.wait_ge(S["q_normed"], S.at("q_normed", 3))
                if h >= 2:
                    pe.wait_ge(S["decay_operands"], S.at("decay_operands", h - 2))
                pe.matmul(PS[:, 6 + h % 2, :], bc(IDENT[0:DH, h:h + 1], [DH, P]), ROWS[0:DH, :, :], start=True, stop=True).then_inc(S["row_spread"], S.mark("row_spread", h))
                if h >= 2:
                    pe.wait_ge(S["kk_taken"], S.at("kk_taken", h - 2))
                for c in range(2):
                    cs = slice(c * P, (c + 1) * P)
                    pe.matmul(PS[:, h % 2, cs], KD3[:, h, cs], KD3[:, h, cs], start=True, stop=True)
                for c in range(2):
                    cs = slice(c * P, (c + 1) * P)
                    ins = pe.matmul(PS[:, h % 2, T + c * P:T + (c + 1) * P], KD3[:, h, cs], QD[:, h, cs], start=True, stop=True)
                ins.then_inc(S["kk"], S.mark("kk", h))
            pe.wait_ge(S["kk_taken"], S.at("kk_taken", 7))
            pe.wait_ge(S["side_taken"], S.at("side_taken", 7))
            for lv in range(LV3):
                for g in range(4):
                    pe.wait_ge(S["masked_l"], S.at("masked_l", (lv, g)))
                    if lv:
                        pe.wait_ge(S["inverse"], S.at("inverse", (lv - 1, g)))
                    if lv or g >= 2:
                        pe.wait_ge(S["product_taken"], S.at("product_taken", (lv, g - 2) if g >= 2 else (lv - 1, g + 2)))
                    for u in range(4 * g, 4 * g + 4):
                        us = unit(u)[1]
                        ins = pe.matmul(PS[:, g % 2, us], CT[:, g, us], XI[:, g, us] if lv else IDENT, start=True, stop=True)
                    ins.then_inc(S["product"], S.mark("product", (lv, g)))
                if lv == 0:
                    continue
                for g in range(4):
                    pe.wait_ge(S["product_taken"], S.at("product_taken", (lv, g)))
                    if lv > 1 or g >= 2:
                        pe.wait_ge(S["inverse"], S.at("inverse", (lv, g - 2) if g >= 2 else (lv - 1, g + 2)))
                    for u in range(4 * g, 4 * g + 4):
                        us = unit(u)[1]
                        if lv < LV3 - 1:
                            pe.matmul(PS[:, 2 + g % 2, us], XT[:, g, us], ZT[:, g, us], start=True, stop=True)
                    for u in range(4 * g, 4 * g + 4):
                        us = unit(u)[1]
                        ins = pe.matmul(PS[:, 4 + g % 2, us], ZT[:, g, us], XT[:, g, us], start=True, stop=True)
                    ins.then_inc(S["increments3"], S.mark("increments3", (lv, g)))
            for c in range(2):
                for q in range(2):
                    hs = range(4 * q, 4 * q + 4)
                    col = lambda h: slice((h % 4) * P, (h % 4 + 1) * P)
                    if c:
                        pe.wait_ge(S["state3"], S.at("state3", q))
                        for h in hs:
                            ins = pe.matmul(PS[:, q, col(h)], KBG[:, h, P:T], ST3[:, h * P:(h + 1) * P], start=True, stop=True)
                        ins.then_inc(S["recalled"], S.mark("recalled", q))
                        pe.wait_ge(S["rhs3"], S.at("rhs3", q))
                    else:
                        pe.wait_ge(S["inverse"], S.at("inverse", (LV3 - 1, 3)))
                    for h in hs:
                        g, us = unit(2 * h + c)
                        rhs = RV[:, 0, h * P:(h + 1) * P] if c else VB[:, 2 * h, :]
                        ins = pe.matmul(PS[:, 2 + q, col(h)], XT[:, g, us], rhs, start=True, stop=True)
                    ins.then_inc(S["new_values"], S.mark("new_values", (c, q)))
                for q in range(2):
                    hs = range(4 * q, 4 * q + 4)
                    col = lambda h: slice((h % 4) * P, (h % 4 + 1) * P)
                    pe.wait_ge(S["new_values_taken"], S.at("new_values_taken", (c, q)))
                    for h in hs:
                        o = PS[:, 4 + h // 2, (h % 2) * T + c * P:(h % 2) * T + (c + 1) * P]
                        v = RV[:, 1, h * P:(h + 1) * P]
                        if c:
                            pe.matmul(o, ST3[:, h * P:(h + 1) * P], QG[:, h, P:T], start=True, stop=False)
                        ins = pe.matmul(o, v, AT[:, h, c * P:(c + 1) * P], start=not c, stop=True)
                    if c == 0:
                        for h in hs:
                            ins = pe.matmul(PS[:, q, col(h)], KDEC[:, 2 * h, :], RV[:, 1, h * P:(h + 1) * P], start=True, stop=True)
                        ins.then_inc(S["state_product"], S.mark("state_product", q))
            ins.then_inc(S["delta_mixed"], S.mark("delta_mixed"))
            for u in range(4):
                pe.wait_ge(S["o3_squares"], S.at("o3_squares", u))
                pe.matmul(PS[:, u, :], ONES, SQ[:, u, :], start=True, stop=True).then_inc(S["o3_sums"], S.mark("o3_sums", u))
            pe.wait_ge(S["cat3"], S.at("cat3"))
            for i in range(4):
                pe_chunk_tokens_move(pe, START["mix3_out"] + i, OD, slice(0, T), i, T)

        def act_mix3(act, order):
            n0 = START["mix3_in"]
            act.wait_ge(S["logits"], S.at("logits"))
            act.activation(BROW, PS[0:DH, 7, 0:T], ACT.Sigmoid).then_inc(S["beta3"], S.mark("beta3"))
            act.activation(W8[0:DH, 1, :], PS[0:DH, 7, T:T2], ACT.Identity, bias=sm("dt_bias")[0:DH, :]).then_inc(order.sem, order.step())
            act.wait_ge(order.sem, order.n)
            act.activation(W8[0:DH, 2, :], W8[0:DH, 1, :], ACT.Abs).then_inc(order.sem, order.step())
            act.wait_ge(order.sem, order.n)
            act.activation(W8[0:DH, 2, :], W8[0:DH, 2, :], ACT.Exp, scale=-1.0).then_inc(order.sem, order.step())
            act.wait_ge(order.sem, order.n)
            act.activation(W8[0:DH, 2, :], W8[0:DH, 2, :], ACT.Ln, bias=EPS[0:DH, 2:3]).then_inc(order.sem, order.step())
            act.wait_ge(order.sem, order.n)
            act.activation(NA[:, 0:1], sm("a_log")[0:DH, :], ACT.Exp).then_inc(S["decay_rate"], S.mark("decay_rate"))
            act.wait_ge(S["left3"], S.at("left3"))
            act.activation(W8[0:DH, 0, :], W8[0:DH, 0, :], ACT.Exp).then_inc(S["rows3"], S.mark("rows3"))
            for i in range(12):
                act.wait_ge(S["conv3"], S.at("conv3", i))
                x = QKV[:, 2 * i:2 * i + 2, :]
                act.activation(x, x, ACT.Silu).then_inc(S["conv_silu"], S.mark("conv_silu", i))
            for i in range(12, 16):
                need_product(act, n0 + i)
                act.activation(flat(ZS[:, 2 * i - 24:2 * i - 22, :]), PS[:, i % 6, :], ACT.Silu).then_inc(S["z_taken"], S.mark("z_taken", i))
            act.wait_ge(S["conv_silu"], S.at("conv_silu", 7))
            for i in range(8):
                act.activation(SQ[:, i, :].rearrange("p (a b) -> p a b", a=2), QKV[:, 2 * i:2 * i + 2, :], ACT.Square).then_inc(S["qk_squares"], S.mark("qk_squares", i))
            for u in range(8):
                act.wait_ge(S["qk_sums"], S.at("qk_sums", u))
                act.activation(RN3[:, u, :], PS[:, (0, 1, 2, 3, 4, 5, 0, 1)[u], :], ACT.Ln, bias=EPS[:, 0:1]).then_inc(order.sem, order.step())
                act.wait_ge(order.sem, order.n)
                act.activation(RN3[:, u, :], RN3[:, u, :], ACT.Exp, scale=-0.5).then_inc(S["qk_rinv"], S.mark("qk_rinv", u))
            act.wait_ge(S["cols_taken"], S.at("cols_taken"))
            for i in range(8):
                act.wait_ge(S["side_turned"], S.at("side_turned", i))
                which, g = i // 4, i % 4
                for u in range(4 * g, 4 * g + 4):
                    ins = act.activation((VB, KDEC)[which][:, u, :], PS[:, 2 + g, unit(u)[1]], ACT.Identity,
                                         scale=COLS[:, u % 2, 1 + which, u // 2:u // 2 + 1])
                    if u % 4 < 3:
                        ins.then_inc(order.sem, order.step())
                ins.then_inc(S["side_taken"], S.mark("side_taken", i))
            for h in range(DH):
                act.wait_ge(S["row_spread"], S.at("row_spread", h))
                act.activation(KBG[:, h, :], PS[:, 6 + h % 2, 0:T], ACT.Exp).then_inc(S["row_exp"], S.mark("row_exp", h))
                act.wait_ge(S["differences"], S.at("differences", h))
                act.activation(DM[:, h, :], DM[:, h, :], ACT.Exp).then_inc(S["decays"], S.mark("decays", h))
            for lv in range(LV3):
                for g in range(4):
                    act.wait_ge(S["product"], S.at("product", (lv, g)))
                    if lv > 1:
                        act.wait_ge(S["increments3"], S.at("increments3", (lv - 1, g)))
                    act.activation(ZT[:, g, :], PS[:, g % 2, :], ACT.Identity).then_inc(S["product_taken"], S.mark("product_taken", (lv, g)))
            for c in range(2):
                for q in range(2):
                    act.wait_ge(S["new_values"], S.at("new_values", (c, q)))
                    if c:
                        act.wait_ge(S["rhs3"], S.at("rhs3", 1))
                    act.activation(RV[:, 1, q * 512:(q + 1) * 512], PS[:, 2 + q, :], ACT.Identity).then_inc(S["new_values_taken"], S.mark("new_values_taken", (c, q)))
            act.wait_ge(S["delta_mixed"], S.at("delta_mixed"))
            for u in range(4):
                act.activation(SQ[:, u, :], PS[:, 4 + u, :], ACT.Square).then_inc(S["o3_squares"], S.mark("o3_squares", u))
            for u in range(4):
                act.wait_ge(S["o3_sums"], S.at("o3_sums", u))
                act.activation(SQ[:, 4 + u, :], PS[:, u, :], ACT.Ln, scale=1.0 / P, bias=EPS[:, 0:1]).then_inc(order.sem, order.step())
                act.wait_ge(order.sem, order.n)
                act.activation(SQ[:, 4 + u, :], SQ[:, 4 + u, :], ACT.Exp, scale=-0.5).then_inc(S["o3_rinv"], S.mark("o3_rinv", u))

        def dve_mix3(dve, order):
            n0 = START["mix3_in"]
            dve.wait_ge(S["decay_rate"], S.at("decay_rate"))
            dve.tensor_scalar(NA[:, 1:2], NA[:, 0:1], -1.0, None, ALU.mult).then_inc(order.sem, order.step())
            dve.wait_ge(order.sem, order.n)
            dve.scalar_tensor_tensor(out=W8[0:DH, 3, :], in0=W8[0:DH, 1, :], scalar=0.0, in1=W8[0:DH, 2, :],
                                               op0=ALU.max, op1=ALU.add).then_inc(order.sem, order.step())
            dve.wait_ge(order.sem, order.n)
            dve.tensor_scalar(W8[0:DH, 3, :], W8[0:DH, 3, :], NA[:, 1:2], None, ALU.mult).then_inc(order.sem, order.step())
            dve.wait_ge(order.sem, order.n)
            dve.memset(W8[0:DH, 1, :], 1.0).then_inc(order.sem, order.step())
            dve.wait_ge(order.sem, order.n)
            for c in range(2):
                cs = slice(c * P, (c + 1) * P)
                dve.tensor_tensor_scan(GROW[:, cs], W8[0:DH, 1, cs], W8[0:DH, 3, cs], 0.0, ALU.mult, ALU.add).then_inc(order.sem, order.step())
                dve.wait_ge(order.sem, order.n)
            last = bc(GROW.rearrange("p (c t) -> p c t", c=2)[:, :, P - 1:P], [DH, 2, P])
            dve.tensor_tensor(W8[0:DH, 0, :].rearrange("p (c t) -> p c t", c=2), last,
                                     GROW.rearrange("p (c t) -> p c t", c=2), ALU.subtract).then_inc(S["left3"], S.mark("left3"))
            for i in range(12):
                need_product(dve, n0 + i)
                for t in range(2):
                    m = 2 * i + t
                    x = PS[:, i % 6, t * T:(t + 1) * T]
                    tap = lambda j: sm("c_conv")[:, j * 24 + m:j * 24 + m + 1]
                    dve.tensor_scalar(QKV[:, m, :], x, tap(3), None, ALU.mult).then_inc(order.sem, order.step())
                for j in (2, 1, 0):
                    dve.wait_ge(order.sem, order.n)
                    for t in range(2):
                        m, lag = 2 * i + t, 3 - j
                        x = PS[:, i % 6, t * T:(t + 1) * T]
                        ins = dve.scalar_tensor_tensor(out=QKV[:, m, lag:], in0=x[:, 0:T - lag], scalar=sm("c_conv")[:, j * 24 + m:j * 24 + m + 1],
                                                       in1=QKV[:, m, lag:], op0=ALU.mult, op1=ALU.add)
                        if (j, t) == (0, 1):
                            ins.then_inc(S["conv3"], S.mark("conv3", i))
                        else:
                            ins.then_inc(order.sem, order.step())
            dve.wait_ge(S["cols3"], S.at("cols3"))
            dve.tensor_copy(COLS.rearrange("p c j h -> p (c j h)"), PS[:, 7, 0:6 * DH]).then_inc(S["cols_taken"], S.mark("cols_taken"))
            for u in range(8):
                dve.wait_ge(S["qk_rinv"], S.at("qk_rinv", u))
                x = QKV[:, 2 * u:2 * u + 2, :]
                r = RN3[:, u, :].rearrange("p (a b) -> p a b", a=2)
                if u < 4:
                    dve.scalar_tensor_tensor(out=x, in0=x, scalar=QUERY_SCALE, in1=r, op0=ALU.mult, op1=ALU.mult).then_inc(S["q_normed"], S.mark("q_normed", u))
                else:
                    dve.tensor_tensor(x, x, r, ALU.mult).then_inc(S["k_normed"], S.mark("k_normed", u - 4))
            causal = bc(CAUSAL.unsqueeze(1), [P, 2, P])
            halves3 = lambda ap: ap.rearrange("p (c t) -> p c t", c=2)
            for h in range(DH):
                dve.wait_ge(S["row_spread"], S.at("row_spread", h))
                dve.wait_ge(S["row_exp"], S.at("row_exp", h))
                for c in range(2):
                    ins = dve.tensor_scalar(DM[:, h, c * P:(c + 1) * P], PS[:, 6 + h % 2, c * P:(c + 1) * P],
                                            COLS[:, c, 0, h:h + 1], 0.0, ALU.subtract, ALU.min)
                    if c == 0:
                        ins.then_inc(order.sem, order.step())
                ins.then_inc(S["differences"], S.mark("differences", h))
                dve.tensor_tensor(QG[:, h, :], QD[:, h, :], KBG[:, h, :], ALU.mult).then_inc(order.sem, order.step())
                dve.tensor_tensor(KBG[:, h, :], KD3[:, h, :], KBG[:, h, :], ALU.mult).then_inc(order.sem, order.step())
                dve.wait_ge(order.sem, order.n)
                dve.tensor_tensor(KBG[:, h, :], KBG[:, h, :], PS[:, 6 + h % 2, T:T2], ALU.mult).then_inc(order.sem, order.step())
                dve.wait_ge(S["decays"], S.at("decays", h))
                dve.tensor_tensor(halves3(DM[:, h, :]), halves3(DM[:, h, :]), causal, ALU.mult).then_inc(order.sem, order.step())
                dve.wait_ge(order.sem, order.n)
                dve.tensor_tensor(LT[:, h, :], DM[:, h, :], PS[:, 6 + h % 2, T:T2], ALU.mult).then_inc(S["decay_operands"], S.mark("decay_operands", h))
                dve.wait_ge(S["decay_operands"], S.at("decay_operands", h))
                dve.wait_ge(S["kk"], S.at("kk", h))
                dve.tensor_tensor(LT[:, h, :], LT[:, h, :], PS[:, h % 2, 0:T], ALU.mult).then_inc(order.sem, order.step())
                dve.tensor_tensor(AT[:, h, :], DM[:, h, :], PS[:, h % 2, T:T2], ALU.mult).then_inc(S["kk_taken"], S.mark("kk_taken", h))
            dve.wait_ge(S["kk_taken"], S.at("kk_taken", DH - 1))
            lt4 = LT.rearrange("p (g a) t -> p g (a t)", g=4)
            dve.wait_ge(S["negm_loaded"], S.at("negm_loaded"))
            ident4 = bc(IDENT.unsqueeze(1), [P, 4, P])
            by4 = lambda ap: ap.rearrange("p (u t) -> p u t", t=P)

            def mask(lv, g):
                if lv:
                    dve.wait_ge(S["product"], S.at("product", (lv - 1, g)))
                m = bc(NEGL[:, lv // 2, (lv % 2) * P:(lv % 2 + 1) * P].unsqueeze(1), [P, 4, P])
                dve.tensor_tensor(by4(CT[:, g, :]), by4(lt4[:, g, :]), m, ALU.mult).then_inc(S["masked_l"], S.mark("masked_l", (lv, g)))

            for g in range(4):
                mask(0, g)
            for g in range(4):
                dve.wait_ge(S["product_taken"], S.at("product_taken", (0, g)))
                dve.tensor_tensor(by4(XI[:, g, :]), by4(ZT[:, g, :]), ident4, ALU.add).then_inc(order.sem, order.step())
                dve.wait_ge(S["masked_l"], S.at("masked_l", (0, g)))
                dve.tensor_tensor(by4(XT[:, g, :]), by4(CT[:, g, :]), ident4, ALU.add).then_inc(S["inverse"], S.mark("inverse", (0, g)))
            for lv in range(1, LV3):
                for g in range(4):
                    if lv == 1:
                        dve.wait_ge(S["inverse"], S.at("inverse", (0, g)))
                    mask(lv, g)
                for g in range(4):
                    dve.wait_ge(S["increments3"], S.at("increments3", (lv, g)))
                    if lv < LV3 - 1:
                        dve.tensor_tensor(XI[:, g, :], XI[:, g, :], PS[:, 2 + g % 2, :], ALU.add).then_inc(order.sem, order.step())
                    dve.tensor_tensor(XT[:, g, :], XT[:, g, :], PS[:, 4 + g % 2, :], ALU.add).then_inc(S["inverse"], S.mark("inverse", (lv, g)))
            for q in range(2):
                dve.wait_ge(S["state_product"], S.at("state_product", q))
                dve.tensor_copy(ST3[:, q * 512:(q + 1) * 512], PS[:, q, :]).then_inc(S["state3"], S.mark("state3", q))
            for q in range(2):
                dve.wait_ge(S["recalled"], S.at("recalled", q))
                vb = VB.rearrange("p (h c) n -> p h c n", c=2)[:, 4 * q:4 * q + 4, 1, :]
                dve.tensor_tensor(by4(RV[:, 0, q * 512:(q + 1) * 512]), vb, by4(PS[:, q, :]), ALU.subtract).then_inc(S["rhs3"], S.mark("rhs3", q))
            for u in range(4):
                dve.wait_ge(S["o3_rinv"], S.at("o3_rinv", u))
                o = OD[:, 2 * u:2 * u + 2, :]
                dve.scalar_tensor_tensor(out=flat(o), in0=PS[:, 4 + u, :], scalar=sm("c_norm"), in1=SQ[:, 4 + u, :],
                                                   op0=ALU.mult, op1=ALU.mult).then_inc(order.sem, order.step())
                dve.wait_ge(order.sem, order.n)
                ins = dve.tensor_tensor(o, o, ZS[:, 2 * u:2 * u + 2, :], ALU.mult)
                if u < 3:
                    ins.then_inc(order.sem, order.step())
            ins.then_inc(S["cat3"], S.mark("cat3"))

        block = stack.enter_context(nc.Block())
        PARTS = ["mix0", "layer0", "mix1", "layer1", "preffn2", "mix2", "layer2", "preffn3", "mix3", "layer3"]
        AFTER = {"mix0": "mix0_out", "layer0": "ffn0_ctx", "mix1": "mix1_out", "layer1": "ffn1_lat", "preffn2": "ffn2",
                 "mix2": "mix2_out", "layer2": "ple2", "preffn3": "ffn4", "mix3": "mix3_out", "layer3": "ple3"}
        LASTUSE = START[AFTER[stop or "layer3"]] + dict(STAGES)[AFTER[stop or "layer3"]]
        go = lambda part: stop is None or PARTS.index(part) <= PARTS.index(stop)

        def dve_rest(dve, order):
            if not go("mix1"):
                return
            dve_modulation(dve, order, 1)
            dve_modulate(dve, order, "mix1", BOTH, G_MIX, SH_MIX, (0, 1))
            dve_mix1(dve, order)
            dve_residual(dve, order, "mix1_post", ACC, G_MIXOUT, 0)
            dve.wait_ge(S["residual"], S.at("residual", ("mix1_post", 0)))
            if not go("layer1"):
                return
            dve_modulate(dve, order, "ffn1_pre", LAT, G_FFN, SH_FFN, (0,))
            dve_split_first(dve, "ffn1_lat")
            dve_split_input(dve, "ffn1_lat", H[:, :, LAT])
            dve_ffn(dve, "ffn1_lat")
            dve_residual(dve, order, "ffn1_lat", ACC, G_FFNOUT, 0)
            dve.wait_ge(S["residual"], S.at("residual", ("ffn1_lat", 0)))
            for l in (2, 3):
                if not go(f"preffn{l}"):
                    return
                dve_split_first(dve, f"ffn{2 * l - 2}")
                dve_split_input(dve, f"ffn{2 * l - 2}", XL)
                dve_ffn(dve, f"ffn{2 * l - 2}")
                need_product(dve, START[f"ffn{2 * l - 2}"] + FF_CHUNKS - 1)
                dve_layernorm(dve, order, f"ffn{2 * l - 2}", 0.5, 3 * (l - 2))
                if not go(f"mix{l}"):
                    return
                (dve_mix2 if l == 2 else dve_mix3)(dve, order)
                need_product(dve, START[f"mix{l}_out"] + 3)
                dve_layernorm(dve, order, f"mix{l}", 1.0, 3 * (l - 2) + 1)
                if not go(f"layer{l}"):
                    return
                dve_split_first(dve, f"ffn{2 * l - 1}")
                dve_split_input(dve, f"ffn{2 * l - 1}", XL)
                dve_ffn(dve, f"ffn{2 * l - 1}")
                need_product(dve, START[f"ffn{2 * l - 1}"] + FF_CHUNKS - 1)
                dve_layernorm(dve, order, f"ffn{2 * l - 1}", 0.5, 3 * (l - 2) + 2)
                dve_ple(dve, order, l)

        @block.sync
        def _(sp):
            sp.dma_start(SM[:, :], small).then_inc(S["small_loaded"], S.mark("small_loaded", by=16))
            sp.dma_start(CO[:, :], consts).then_inc(S["consts_loaded"], S.mark("consts_loaded", by=16))
            sp.dma_start(X[:, :, :], xt).then_inc(S["x_loaded"], S.mark("x_loaded", by=16))
            sp.dma_start(MASKS, masks).then_inc(S["masks_loaded"], S.mark("masks_loaded", by=16))
            sp.dma_start(INVC.rearrange("p a b -> p (a b)"), extra["invc"]).then_inc(S["counts_loaded"], S.mark("counts_loaded", by=16))
            again = START["ffn0_ctx"]
            sp_stream(sp, 0, min(LASTUSE, again), 0)
            if LASTUSE > again:
                sp_stream(sp, again, LASTUSE - again, FF_CHUNKS)
            sp.wait_ge(S["finished"], S.at("finished"))
            if stop:
                sp.dma_start(out, X[:, :, :]).then_inc(S["stored"], S.mark("stored", by=16))
            else:
                sp.dma_start(out, X[:, :, LAT]).then_inc(S["stored"], S.mark("stored", by=16))
            sp.wait_ge(S["stored"], S.at("stored"))

        @block.tensor
        def _(pe):
            pe.wait_ge(S["consts_loaded"], S.at("consts_loaded"))
            pe.wait_ge(S["cond_silu"], S.at("cond_silu"))
            pe.wait_ge(S["zeros"], S.at("zeros"))
            pe_ada(pe, 0)
            pe_norm(pe, "mix0", BOTH)
            pe_mix0(pe)
            pe_norm(pe, "mix0_post", BOTH)
            if stop == "mix0":
                return
            pe_norm(pe, "ffn0_pre", BOTH)
            pe_ffn(pe, "ffn0_lat")
            pe_norm(pe, "ffn0_lat", LAT)
            pe.wait_ge(S["residual"], S.at("residual", ("ffn0_lat", 0)))
            pe_ffn(pe, "ffn0_ctx")
            pe_norm(pe, "ffn0_ctx", CTX)
            if not go("mix1"):
                return
            pe.wait_ge(S["residual"], S.at("residual", ("ffn0_ctx", 1)))
            pe_ada(pe, 1)
            pe_norm(pe, "mix1", BOTH)
            pe_mix1(pe)
            pe_norm(pe, "mix1_post", LAT)
            if not go("layer1"):
                return
            pe_norm(pe, "ffn1_pre", LAT)
            pe_ffn(pe, "ffn1_lat")
            pe_norm(pe, "ffn1_lat", LAT)
            if not go("preffn2"):
                return
            pe_ffn(pe, "ffn2")
            pe_layernorm(pe, "ffn2")
            if not go("mix2"):
                return
            pe.wait_ge(S["ln_out"], S.at("ln_out", "ffn2"))
            pe_mix2(pe)
            pe_layernorm(pe, "mix2")
            if not go("layer2"):
                return
            pe_ffn(pe, "ffn3")
            pe_layernorm(pe, "ffn3")
            pe.wait_ge(S["ln_out"], S.at("ln_out", "ffn3"))
            pe_ple(pe, 2)
            if not go("preffn3"):
                return
            pe_ffn(pe, "ffn4")
            pe_layernorm(pe, "ffn4")
            if not go("mix3"):
                return
            pe.wait_ge(S["ln_out"], S.at("ln_out", "ffn4"))
            pe_mix3(pe)
            pe_layernorm(pe, "mix3")
            if not go("layer3"):
                return
            pe_ffn(pe, "ffn5")
            pe_layernorm(pe, "ffn5")
            pe.wait_ge(S["ln_out"], S.at("ln_out", "ffn5"))
            pe_ple(pe, 3)

        @block.scalar
        def _(act):
            order = Order(S["scalar_order"])
            act.wait_ge(S["small_loaded"], S.at("small_loaded"))
            act.activation(CS[:, :, :], sm("cvec").rearrange("p (k s) -> p k s", s=2), ACT.Silu).then_inc(S["cond_silu"], S.mark("cond_silu"))
            act.wait_ge(S["lower_max"], S.at("lower_max"))
            act.activation(TMP[:, 32:48], TMP[:, 32:48], ACT.Exp).then_inc(S["lower_exp"], S.mark("lower_exp"))
            act.wait_ge(S["x_loaded"], S.at("x_loaded"))
            act_squares(act, "mix0", X[:, :, :], BOTH)
            act_rinv(act, order, "mix0", T2, D, 0)
            act_mix0(act, order)
            act.wait_ge(S["taken_out0"], S.at("taken_out0", 3))
            act_squares(act, "mix0_post", Y0, BOTH)
            act_rinv(act, order, "mix0_post", T2, D, 0)
            if stop == "mix0":
                return
            act.wait_ge(S["residual"], S.at("residual", ("mix0_post", 1)))
            act_squares(act, "ffn0_pre", X[:, :, :], BOTH)
            act_rinv(act, order, "ffn0_pre", T2, D, 0)
            for s, tag in ((0, "ffn0_lat"), (1, "ffn0_ctx")):
                act_split_first(act, tag)
                act.wait_ge(S["normed"], S.at("normed", "ffn0_pre"))
                act_split_input(act, tag, H[:, :, STREAM[s]])
                act_ffn(act, tag)
                need_product(act, START[tag] + FF_CHUNKS - 1)
                act_squares(act, tag, ACC, STREAM[s])
                act_rinv(act, order, tag, T, D, 0)
            if not go("mix1"):
                return
            act.wait_ge(S["residual"], S.at("residual", ("ffn0_ctx", 1)))
            act_squares(act, "mix1", X[:, :, :], BOTH)
            act_rinv(act, order, "mix1", T2, D, 0)
            act_mix1(act, order)
            need_product(act, START["mix1_out"] + 3)
            act_squares(act, "mix1_post", ACC, LAT)
            act_rinv(act, order, "mix1_post", T, D, 0)
            if not go("layer1"):
                return
            act.wait_ge(S["residual"], S.at("residual", ("mix1_post", 0)))
            act_squares(act, "ffn1_pre", XL, LAT)
            act_rinv(act, order, "ffn1_pre", T, D, 0)
            act_split_first(act, "ffn1_lat")
            act.wait_ge(S["normed"], S.at("normed", "ffn1_pre"))
            act_split_input(act, "ffn1_lat", H[:, :, LAT])
            act_ffn(act, "ffn1_lat")
            need_product(act, START["ffn1_lat"] + FF_CHUNKS - 1)
            act_squares(act, "ffn1_lat", ACC, LAT)
            act_rinv(act, order, "ffn1_lat", T, D, 0)
            for l in (2, 3):
                if not go(f"preffn{l}"):
                    return
                act_split_first(act, f"ffn{2 * l - 2}")
                if l == 2:
                    act.wait_ge(S["residual"], S.at("residual", ("ffn1_lat", 0)))
                else:
                    act.wait_ge(S["ple_out"], S.at("ple_out", 2))
                act_split_input(act, f"ffn{2 * l - 2}", XL)
                act_ffn(act, f"ffn{2 * l - 2}")
                act_layernorm(act, order, f"ffn{2 * l - 2}")
                if not go(f"mix{l}"):
                    return
                (act_mix2 if l == 2 else act_mix3)(act, order)
                act_layernorm(act, order, f"mix{l}")
                if not go(f"layer{l}"):
                    return
                act_split_first(act, f"ffn{2 * l - 1}")
                act.wait_ge(S["ln_out"], S.at("ln_out", f"mix{l}"))
                act_split_input(act, f"ffn{2 * l - 1}", XL)
                act_ffn(act, f"ffn{2 * l - 1}")
                act_layernorm(act, order, f"ffn{2 * l - 1}")
                act_ple(act, order, l)

        @block.vector
        def _(dve):
            order = Order(S["vector_order"])
            dve.memset(ZERO[:, :], 0.0).then_inc(S["zeros"], S.mark("zeros"))
            for i, v in enumerate((RMS_EPS, LN_EPS / ALPHA2, 1.0)):
                dve.memset(EPS[:, i:i + 1], v).then_inc(order.sem, order.step())
            dve.wait_ge(S["small_loaded"], S.at("small_loaded"))
            lo = sm("lower").rearrange("p (r n) -> p r n", r=2)
            dve.tensor_tensor(TMP[:, 48:56], lo[:, 0, :], lo[:, 1, :], ALU.max).then_inc(order.sem, order.step())
            dve.wait_ge(order.sem, order.n)
            dve.tensor_tensor(TMP[:, 32:40], lo[:, 0, :], TMP[:, 48:56], ALU.subtract).then_inc(order.sem, order.step())
            dve.tensor_tensor(TMP[:, 40:48], lo[:, 1, :], TMP[:, 48:56], ALU.subtract).then_inc(S["lower_max"], S.mark("lower_max"))
            dve.wait_ge(S["lower_exp"], S.at("lower_exp"))
            dve.tensor_tensor(TMP[:, 48:56], TMP[:, 32:40], TMP[:, 40:48], ALU.add).then_inc(order.sem, order.step())
            dve.wait_ge(order.sem, order.n)
            dve.reciprocal(TMP[:, 48:56], TMP[:, 48:56]).then_inc(order.sem, order.step())
            dve.wait_ge(order.sem, order.n)
            dve.tensor_tensor(TMP[:, 32:40], TMP[:, 32:40], TMP[:, 48:56], ALU.mult).then_inc(order.sem, order.step())
            dve.tensor_tensor(TMP[:, 40:48], TMP[:, 40:48], TMP[:, 48:56], ALU.mult).then_inc(order.sem, order.step())
            dve.wait_ge(S["masks_loaded"], S.at("masks_loaded"))
            dve.tensor_copy(M8[:, :], MASKS).then_inc(S["masks_ready"], S.mark("masks_ready"))
            dve_modulation(dve, order, 0)
            dve_modulate(dve, order, "mix0", BOTH, G_MIX, SH_MIX, (0, 1))
            dve.wait_ge(S["masks_ready"], S.at("masks_ready"))
            dve.wait_ge(S["consts_loaded"], S.at("consts_loaded"))
            dve_mix0(dve, order)
            dve_residual(dve, order, "mix0_post", Y0[:, :, LAT], G_MIXOUT, 0, T)
            dve_residual(dve, order, "mix0_post", Y0[:, :, CTX], G_MIXOUT, 1, 0)
            if stop == "mix0":
                dve.wait_ge(S["residual"], S.at("residual", ("mix0_post", 1)))
                dve.memset(TMP[:, 62:63], 0.0).then_inc(S["finished"], S.mark("finished"))
                return
            dve_modulate(dve, order, "ffn0_pre", BOTH, G_FFN, SH_FFN, (0, 1))
            for s, tag in ((0, "ffn0_lat"), (1, "ffn0_ctx")):
                dve_split_first(dve, tag)
                dve_split_input(dve, tag, H[:, :, STREAM[s]])
                dve_ffn(dve, tag)
                dve_residual(dve, order, tag, ACC, G_FFNOUT, s)
            dve.wait_ge(S["residual"], S.at("residual", ("ffn0_ctx", 1)))
            dve_rest(dve, order)
            dve.memset(TMP[:, 62:63], 0.0).then_inc(S["finished"], S.mark("finished"))

        @block.gpsimd
        def _(pool):
            order = Order(S["pool_order"])
            pool_mix0(pool, order)
            if not go("mix1"):
                return
            pool.wait_ge(S["residual"], S.at("residual", ("mix0_post", 1)))
            pool.dma_start(AR[:, 7168:7680], extra["rope"]).then_inc(S["rope_loaded"], S.mark("rope_loaded", by=16))
            pemb = PEMB.rearrange("p l k t -> p (l k t)")
            pool.dma_start(pemb, extra["pt"]).then_inc(S["emb_loaded"], S.mark("emb_loaded", 2, by=16))
            if not go("mix2"):
                return
            pool.wait_ge(S["normed"], S.at("normed", "mix1"))
            pool.dma_start(NEGL, extra["negl"]).then_inc(S["negm_loaded"], S.mark("negm_loaded", by=16))
            pool.wait_ge(S["rotated"], S.at("rotated", 4))
            pool.dma_start(BIAS.rearrange("p h n -> p (h n)"), extra["bias"]).then_inc(S["bias_loaded"], S.mark("bias_loaded", by=16))
            pool.wait_ge(S["residual"], S.at("residual", ("ffn1_lat", 0)))
            pool.dma_start(H[:, 0:2, :].rearrange("p a b -> p (a b)"), extra["wax"]).then_inc(S["gates_loaded"], S.mark("gates_loaded", by=16))
            if not go("layer3"):
                return
            pool.wait_ge(S["delta_mixed"], S.at("delta_mixed"))
            pool.dma_start(pemb, extra["pt"]).then_inc(S["emb_loaded"], S.mark("emb_loaded", 3, by=16))
        return S.marks


def tiles(a):
    a = np.asarray(a)
    a = a.reshape(*a.shape[:-1], a.shape[-1] // P, P)
    return np.ascontiguousarray(np.moveaxis(a, -1, 0))


def chunks_in(w):
    k, n = w.shape
    return w.reshape(k // P, P, n // 256, 256).transpose(2, 1, 0, 3).reshape(n // 256, P, -1)


def chunks_out(w):
    return w.reshape(w.shape[0] // 256, 2, P, D).transpose(0, 2, 1, 3).reshape(-1, P, 2 * D)


def chunks_ffn(wg, wu, wd):
    g, u, d = chunks_in(wg), chunks_in(wu), chunks_out(wd)
    order = [g[0], u[0]]
    for i in range(1, FF_STEPS):
        order += [g[i], u[i], d[i - 1]]
    return np.stack(order + [d[FF_STEPS - 1]])


def shape_constants():
    eye, ones = np.eye(P, dtype=np.float32), np.ones((P, P), np.float32)
    rope = np.zeros((P, P), np.float32)
    for p in range(P):
        q = p % 64
        if q < 32:
            rope[p + 32, p] = -1.0
        else:
            rope[p - 32, p] = 1.0
    causal = np.triu(np.ones((P, P), np.float32))
    consts = np.concatenate([eye, ones, rope, causal], 1)
    masks = np.zeros((P, 2 * LEVELS, 256), np.float32)
    s = np.arange(P)
    for lv in range(LEVELS):
        h = 1 << lv
        for d in range(2):
            qpos = (s.reshape(-1, 2, h)[:, 1 - d, :]).reshape(-1)
            same = s[:, None] // (2 * h) == qpos[None, :] // (2 * h)
            in_k = ((s // h) % 2 == d)[:, None]
            masks[:, 2 * lv + d] = np.tile((same & in_k).astype(np.float32), (1, NCH))
    t = np.arange(T)
    inv = np.stack([1.0 / (np.clip(t - w // 2 + w, 0, T) - np.clip(t - w // 2, 0, T)) for w in (2, 4, 8, 16)])
    invc = np.broadcast_to(inv.astype(np.float32).reshape(1, -1), (P, 4 * T)).copy()
    n_freq, width = 32, 64
    freq = 10000.0 ** (-np.arange(n_freq) / n_freq)
    pos = np.stack([t // width, t % width])
    ang = np.concatenate([np.tile(pos[a][None, :] * freq[:, None], (2, 1)) for a in range(2)], 0)
    ropes = np.concatenate([np.cos(ang), np.sin(ang)], 1).astype(np.float32)
    bias = np.zeros((P, 8, 384), np.float32)
    for half, (at, keys) in enumerate(((0, P), (P, T))):
        q, k = np.arange(P)[:, None] + half * P, np.arange(keys)[None, :]
        reach = (k // 64 <= q // 64) & (k // 64 >= q // 64 - 2)
        for h in range(8):
            bias[:, h, at:at + keys] = np.where(reach, -(2.0 ** -(h + 1)) * np.abs(q - k), -1e30)
    negl = np.zeros((P, 8, P), np.float32)
    for lv in range(LEVELS):
        h = 1 << lv
        j, i = s[:, None], s[None, :]
        negl[:, lv] = -((j // (2 * h) == i // (2 * h)) & ((j // h) % 2 == 0) & ((i // h) % 2 == 1)).astype(np.float32)
    return {"consts": consts, "masks": masks.reshape(P, -1), "invc": invc, "rope": ropes,
            "bias": bias.reshape(P, -1), "negl": negl.reshape(P, 4, 256)}


def lay_out(inputs):
    g = {k: np.asarray(v) for k, v in inputs.items()}
    parts = {}
    cut = lambda w, lo, n: w[:, lo:lo + n]
    z = g["ab_w_in"][0]
    w0 = np.concatenate([cut(z, 512, 512), cut(z, 2560, 512), cut(z, 1024, 1024), cut(z, 2048, 512), cut(z, 0, 512)], 1)
    for l in range(2):
        parts[f"ada{l}"] = chunks_in(g["ada_w"][l])
        parts["ffn0_lat" if l == 0 else "ffn1_lat"] = chunks_ffn(g["ffn_w_in"][l][:, :FF], g["ffn_w_in"][l][:, FF:], g["ffn_w_out"][l])
    parts["mix0_in"] = chunks_in(w0)
    parts["mix0_out"] = chunks_in(g["ab_w_out"][0])
    a = g["att_w_in"][0]
    parts["mix1_in"] = chunks_in(np.concatenate([a[:, 1024:], a[:, :1024]], 1))
    parts["mix1_out"] = chunks_in(g["att_w_out"][0])
    for l in range(2):
        for i, n in ((1, f"ffn{2 + 2 * l}"), (2, f"ffn{3 + 2 * l}")):
            parts[n] = chunks_ffn(g[f"ffn{i}_wg_2"][l], g[f"ffn{i}_wu_2"][l], g[f"ffn{i}_wd_2"][l])
        wp = g["ple_wp_2"][l].reshape(2, P, D).transpose(1, 0, 2).reshape(1, P, -1)
        parts[f"ple{2 + l}"] = np.concatenate([chunks_in(g["ple_wg_2"][l]), wp])
    heads = np.arange(8).reshape(2, 4).T.reshape(-1)
    perm = (heads[:, None] * 64 + np.arange(64)).reshape(-1)
    w = g["ab_w_in_2"][0]
    parts["mix2_in"] = chunks_in(np.concatenate([w[:, 512:768], w[:, :512][:, perm], w[:, 768:]], 1))
    wo = g["ab_w_out_2"][0]
    parts["mix2_out"] = chunks_in(np.concatenate([wo[:512][perm], wo[512:]], 0))
    parts["mix3_in"] = chunks_in(g["c_w_in_2"][0][:, :4096])
    parts["mix3_out"] = chunks_in(g["c_w_out_2"][0])
    stream = np.concatenate([parts[n] for n, _ in STAGES if n != "ffn0_ctx"])
    assert stream.shape == (N_CHUNKS, P, CHUNK_COLS)

    small = np.zeros((P, SMALL_COLS), np.float32)
    put = lambda name, a: small.__setitem__((slice(0, a.shape[0]), SMALL[name]), a.reshape(a.shape[0], -1))
    put("cvec", np.moveaxis(tiles(np.stack([g["c"][0], g["c_ctx"]])), 1, 2))
    put("ada_b", tiles(g["ada_b"]))
    put("norm_g", tiles(g["norm_g"]))
    put("lower", tiles(g["hg_lower"]))
    put("pool_scale", tiles(g["pool_scale"][0]))
    put("onorm", tiles(g["hg_onorm_g"][0]))
    put("qnorm", tiles(g["att_qnorm_g"][0]))
    put("knorm", tiles(g["att_knorm_g"][0]))
    put("ln_g", tiles(g["ln_g_2"]))
    put("ln_b", tiles(g["ln_b_2"]))
    put("ple_bg", tiles(g["ple_bg_2"]))
    for name, key in (("conv_b", "b_conv_b_2"), ("b_ba", "b_ba_2"), ("b_bx", "b_bx_2"), ("b_lam", "b_lam_2"),
                      ("b_conv", "b_conv_w_2"), ("c_conv", "c_conv_w_2"), ("c_norm", "c_norm_g_2")):
        put(name, tiles(g[key][0]))
    put("sinks", np.broadcast_to(g["a_sinks_2"][0][None, :], (P, 8)))
    put("a_log", g["c_a_log_2"][0][:, None])
    put("dt_bias", g["c_dt_bias_2"][0][:, None])
    put("w_ba", g["c_w_in_2"][0][:, 4096:].reshape(DT, P, 16).transpose(1, 0, 2))
    put("pool_w", g["pool_w"][0].transpose(1, 0, 2))
    x = np.stack([g["ctx"][0], g["x"][0]])
    xt = x.reshape(T2, DT, P).transpose(2, 1, 0)
    pt = np.ascontiguousarray(g["p_2"][:, 0].reshape(2, T, 2, P).transpose(3, 0, 2, 1)).reshape(P, -1)
    wax = np.zeros((P, 2, 4, P), np.float32)
    for i, name in enumerate(("b_wa_2", "b_wx_2")):
        for b in range(8):
            o = 64 * (b % 2)
            wax[o:o + 64, i, b // 2, o:o + 64] = g[name][0, b]
    return {"stream": stream, "small": small, "xt": np.ascontiguousarray(xt), "pt": pt, "wax": wax.reshape(P, -1),
            **shape_constants()}


def program(nc, arrays, out_shape, counts=None, stop=None):
    aps = {n: nc.dram_tensor(n, a.shape, mybir.dt.from_np(a.dtype), kind="ExternalInput").ap() for n, a in arrays.items()}
    out = nc.dram_tensor("out", out_shape, F32, kind="ExternalOutput").ap()
    extra = {n: aps[n] for n in aps if n not in ("stream", "small", "xt", "consts", "masks")}
    marks = build(nc, aps["stream"], aps["small"], aps["xt"], aps["consts"], aps["masks"], extra, out, counts, stop)
    return marks


def kernel(**inputs):
    import concourse.bacc as _bacc
    from concourse.bass_utils import run_bass_kernel_spmd as _run

    arrays = lay_out(inputs)
    shape = (P, DT, T)
    counts = program(_bacc.Bacc("TRN2", target_bir_lowering=False, num_devices=1), arrays, shape)
    nc = _bacc.Bacc("TRN2", target_bir_lowering=False, num_devices=1)
    program(nc, arrays, shape, counts)
    r = _run(nc, [arrays], core_ids=[0])
    y = r.results[0]["out"]
    return np.ascontiguousarray(y.transpose(2, 1, 0)).reshape(1, T, D)
```
